# Optimizing a Trainium2 kernel written in Bass

```python
import jax
import jax.numpy as jnp
from jax import lax
import numpy as np
import math

D_MODEL = 1024
BATCH = 1
SEQ = 512
DEPTH = 1

HEAD_DIM = 64
N_HEADS_A = 4
N_HEADS_C = 4
N_HEADS_D = 4
CONV_CH = 4 * HEAD_DIM
CONV_K = 3
MIX_WIDTH = (N_HEADS_A + N_HEADS_C + N_HEADS_D) * HEAD_DIM + CONV_CH
N_GROUPS = MIX_WIDTH // HEAD_DIM
BLOCK = 128
CMP_LEN = 32
CMP_STRIDE = 16
CMP_HIDDEN = 256
SEL_BLOCK = 64
N_SELECT = 16
NSA_WINDOW = 512
N_NSA_BRANCH = 3
DILATED_CONFIGS = ((128, 1), (512, 4), (2048, 16))
D_FF = -(-(8 * D_MODEL) // (3 * 256)) * 256
A_COLS = N_HEADS_A * HEAD_DIM + 6 * HEAD_DIM + N_NSA_BRANCH * N_HEADS_A
IN_COLS = A_COLS + 3 * CONV_CH + 3 * N_HEADS_C * HEAD_DIM + 3 * N_HEADS_D * HEAD_DIM
COL_WIDTHS = (N_HEADS_A * HEAD_DIM, HEAD_DIM, HEAD_DIM, HEAD_DIM, HEAD_DIM, HEAD_DIM, HEAD_DIM,
              N_NSA_BRANCH * N_HEADS_A,
              CONV_CH, CONV_CH, CONV_CH,
              N_HEADS_C * HEAD_DIM, N_HEADS_C * HEAD_DIM, N_HEADS_C * HEAD_DIM,
              N_HEADS_D * HEAD_DIM, N_HEADS_D * HEAD_DIM, N_HEADS_D * HEAD_DIM)
NEG_INF = -1e30
FORCE_SCORE = 1e6
RMS_EPS = 1e-6


def rms_norm(x, g):
    xf = x.astype(jnp.float32)
    y = xf * lax.rsqrt(jnp.mean(xf * xf, axis=-1, keepdims=True) + RMS_EPS)
    return (y * g.astype(jnp.float32)).astype(x.dtype)

def to_heads(t, n):
    b, s, _ = t.shape
    return t.reshape(b, s, n, HEAD_DIM).transpose(0, 2, 1, 3)

def alibi_slopes(n):
    return jnp.exp2(-8.0 * jnp.arange(1, n + 1, dtype=jnp.float32) / n)

def banded_attention(q, k, v, max_back, dist_scale, slopes):
    n, h, l, hd = q.shape
    g = k.shape[1]
    r = h // g
    nb = l // BLOCK
    n_prev = -(-max_back // BLOCK)
    w = (n_prev + 1) * BLOCK
    qb = q.reshape(n, g, r, nb, BLOCK, hd)

    def band(t):
        tb = t.reshape(n, g, nb, BLOCK, hd)
        tp = jnp.pad(tb, ((0, 0), (0, 0), (n_prev, 0), (0, 0), (0, 0)))
        return jnp.concatenate([tp[:, :, i:i + nb] for i in range(n_prev + 1)], axis=3)

    kb, vb = band(k), band(v)
    rows = jnp.arange(BLOCK)
    diff = rows[:, None] + n_prev * BLOCK - jnp.arange(w)[None, :]
    key_idx = jnp.arange(nb)[:, None, None] * BLOCK + rows[None, :, None] - diff[None]
    mask = (diff >= 0) & (diff <= max_back) & (key_idx >= 0)
    s = jnp.einsum('ngrbqd,ngbkd->ngrbqk', qb, kb).astype(jnp.float32) * (HEAD_DIM ** -0.5)
    s = s - slopes.reshape(g, r)[None, :, :, None, None, None] * (diff * dist_scale).astype(jnp.float32)
    s = jnp.where(mask, s, NEG_INF)
    lse = jax.nn.logsumexp(s, axis=-1)
    p = jnp.exp(s - lse[..., None])
    o = jnp.einsum('ngrbqk,ngbkd->ngrbqd', p.astype(v.dtype), vb)
    return o.reshape(n, h, l, hd), lse.reshape(n, h, l)

def compress_tokens(t, pe, w1, w2):
    b, s, _ = t.shape
    n_cmp = (s - CMP_LEN) // CMP_STRIDE + 1
    idx = jnp.arange(n_cmp)[:, None] * CMP_STRIDE + jnp.arange(CMP_LEN)[None, :]
    blocks = (t[:, idx] + pe).reshape(b, n_cmp, CMP_LEN * HEAD_DIM)
    return jax.nn.gelu(blocks @ w1) @ w2

def nsa_mixer(q_tok, kc_tok, vc_tok, ks_tok, vs_tok, kw_tok, vw_tok, gate_logits, b_gate,
              g_q, g_kc, g_ks, g_kw, pe_k, pe_v, w1_k, w2_k, w1_v, w2_v, slopes):
    b, s, _ = q_tok.shape
    h = N_HEADS_A
    scale = HEAD_DIM ** -0.5
    q = rms_norm(to_heads(q_tok, h), g_q)
    kc = rms_norm(compress_tokens(kc_tok, pe_k, w1_k, w2_k), g_kc)
    vc = compress_tokens(vc_tok, pe_v, w1_v, w2_v)
    n_cmp = kc.shape[1]
    cmp_end = jnp.arange(n_cmp) * CMP_STRIDE + CMP_LEN - 1
    n_sel = s // SEL_BLOCK
    top = min(N_SELECT, n_sel)
    ratio = SEL_BLOCK // CMP_STRIDE
    ks = rms_norm(ks_tok, g_ks).reshape(b, n_sel, SEL_BLOCK, HEAD_DIM)
    vs = vs_tok.reshape(b, n_sel, SEL_BLOCK, HEAD_DIM)
    blk_ids = jnp.arange(n_sel)
    bidx = jnp.arange(b)[:, None, None]
    nc = s // BLOCK
    q_chunks = q.reshape(b, h, nc, BLOCK, HEAD_DIM).transpose(2, 0, 1, 3, 4)

    def chunk(args):
        qi, c = args
        t = c * BLOCK + jnp.arange(BLOCK)
        dist_c = t[:, None] - cmp_end[None, :]
        vis = dist_c >= 0
        sc = jnp.einsum('bhqd,bnd->bhqn', qi, kc).astype(jnp.float32) * scale
        sc = jnp.where(vis, sc - slopes[:, None, None] * dist_c.astype(jnp.float32), NEG_INF)
        p_cmp = jax.nn.softmax(sc, axis=-1) * vis
        o_cmp = jnp.einsum('bhqn,bnd->bhqd', p_cmp.astype(vc.dtype), vc)
        imp = jnp.pad(p_cmp.sum(1), ((0, 0), (0, 0), (0, ratio * n_sel - n_cmp)))
        imp_ov = imp
        for sh in range(1, CMP_LEN // CMP_STRIDE):
            imp_ov = imp_ov + jnp.pad(imp[..., :-sh], ((0, 0), (0, 0), (sh, 0)))
        imp_blk = imp_ov.reshape(b, BLOCK, n_sel, ratio).sum(-1)
        cur = t // SEL_BLOCK
        forced = (blk_ids[None] == 0) | (blk_ids[None] == cur[:, None]) | (blk_ids[None] == cur[:, None] - 1)
        valid = blk_ids[None] * SEL_BLOCK <= t[:, None]
        score = jnp.where(forced, FORCE_SCORE, jnp.where(valid, imp_blk, -FORCE_SCORE))
        _, idx = lax.top_k(score, top)
        kg = ks[bidx, idx]
        vg = vs[bidx, idx]
        pos = idx[..., None] * SEL_BLOCK + jnp.arange(SEL_BLOCK)
        dist_s = t[None, :, None, None] - pos
        ss = jnp.einsum('bhqd,bqkjd->bhqkj', qi, kg).astype(jnp.float32) * scale
        ss = ss - slopes[None, :, None, None, None] * dist_s[:, None].astype(jnp.float32)
        ss = jnp.where((dist_s >= 0)[:, None], ss, NEG_INF)
        p_slc = jax.nn.softmax(ss.reshape(b, h, BLOCK, top * SEL_BLOCK), axis=-1).reshape(ss.shape)
        o_slc = jnp.einsum('bhqkj,bqkjd->bhqd', p_slc.astype(vg.dtype), vg)
        return o_cmp, o_slc

    o_cmp, o_slc = lax.map(chunk, (q_chunks, jnp.arange(nc)))
    o_cmp = o_cmp.transpose(1, 2, 0, 3, 4).reshape(b, h, s, HEAD_DIM)
    o_slc = o_slc.transpose(1, 2, 0, 3, 4).reshape(b, h, s, HEAD_DIM)
    o_win, _ = banded_attention(q, rms_norm(kw_tok, g_kw)[:, None], vw_tok[:, None], NSA_WINDOW - 1, 1, slopes)
    gates = jax.nn.sigmoid(gate_logits + b_gate).reshape(b, s, h, N_NSA_BRANCH).transpose(0, 2, 1, 3)
    return gates[..., 0:1] * o_cmp + gates[..., 1:2] * o_slc + gates[..., 2:3] * o_win

def short_conv_mixer(gate_b, gate_c, u, conv_w):
    y = lax.conv_general_dilated(gate_c * u, conv_w[:, None, :], window_strides=(1,),
                                 padding=[(CONV_K - 1, 0)], dimension_numbers=('NWC', 'WIO', 'NWC'),
                                 feature_group_count=CONV_CH)
    return gate_b * y

def stick_breaking_attention(q, k, v):
    b, h, s, hd = q.shape
    nc = s // BLOCK
    q_chunks = q.reshape(b, h, nc, BLOCK, hd).transpose(2, 0, 1, 3, 4)
    key_pos = jnp.arange(s)

    def chunk(args):
        qi, c = args
        t = c * BLOCK + jnp.arange(BLOCK)
        z = jnp.einsum('bhqd,bhsd->bhqs', qi, k).astype(jnp.float32) * (hd ** -0.5)
        past = key_pos[None, :] < t[:, None]
        neg_log_keep = jnp.where(past, jax.nn.softplus(z), 0.0)
        between = lax.cumsum(neg_log_keep, axis=3, reverse=True) - neg_log_keep
        attn = jnp.where(past, jnp.exp(jax.nn.log_sigmoid(z) - between), 0.0)
        return jnp.einsum('bhqs,bhsd->bhqd', attn.astype(v.dtype), v)

    o = lax.map(chunk, (q_chunks, jnp.arange(nc)))
    return o.transpose(1, 2, 0, 3, 4).reshape(b, h, s, hd)

def dilated_attention(q, k, v, window, dil, slopes):
    b, h, s, hd = q.shape
    span = dil * BLOCK
    sp = -(-s // span) * span
    l = sp // dil

    def fold(t):
        t = jnp.pad(t, ((0, 0), (0, 0), (0, sp - s), (0, 0)))
        return t.reshape(b, h, l, dil, hd).transpose(0, 3, 1, 2, 4).reshape(b * dil, h, l, hd)

    o, lse = banded_attention(fold(q), fold(k), fold(v), window // dil, dil, slopes)
    o = o.reshape(b, dil, h, l, hd).transpose(0, 2, 3, 1, 4).reshape(b, h, sp, hd)[:, :, :s]
    lse = lse.reshape(b, dil, h, l).transpose(0, 2, 3, 1).reshape(b, h, sp)[:, :, :s]
    return o, lse

def hybrid_layer(x, g_mix, w_in, b_gate, g_q_nsa, g_k_cmp, g_k_slc, g_k_win, pe_k_cmp, pe_v_cmp,
                 w1_k_cmp, w2_k_cmp, w1_v_cmp, w2_v_cmp, conv_w, g_q_dil, g_k_dil, g_out, w_out,
                 g_ffn, w_gate, w_up, w_down):
    b, s, _ = x.shape
    hn = rms_norm(x, g_mix)
    proj = hn @ w_in
    cuts = [int(c) for c in np.cumsum(COL_WIDTHS)[:-1]]
    (qa, kca, vca, ksa, vsa, kwa, vwa, gta, cvb, cvc, cvu,
     qc, kc, vc, qd, kd, vd) = jnp.split(proj, cuts, axis=-1)
    slopes = alibi_slopes(N_HEADS_A + N_HEADS_D)
    slopes_a, slopes_d = slopes[0::2], slopes[1::2]
    o_a = nsa_mixer(qa, kca, vca, ksa, vsa, kwa, vwa, gta, b_gate, g_q_nsa, g_k_cmp, g_k_slc, g_k_win,
                    pe_k_cmp, pe_v_cmp, w1_k_cmp, w2_k_cmp, w1_v_cmp, w2_v_cmp, slopes_a)
    o_b = short_conv_mixer(cvb, cvc, cvu, conv_w).reshape(b, s, CONV_CH // HEAD_DIM, HEAD_DIM)
    o_c = stick_breaking_attention(to_heads(qc, N_HEADS_C), to_heads(kc, N_HEADS_C), to_heads(vc, N_HEADS_C))
    qdh = rms_norm(to_heads(qd, N_HEADS_D), g_q_dil)
    kdh = rms_norm(to_heads(kd, N_HEADS_D), g_k_dil)
    vdh = to_heads(vd, N_HEADS_D)
    outs, lses = [], []
    for window, dil in DILATED_CONFIGS:
        o_i, lse_i = dilated_attention(qdh, kdh, vdh, window, dil, slopes_d)
        outs.append(o_i)
        lses.append(lse_i)
    mix_w = jax.nn.softmax(jnp.stack(lses, axis=0), axis=0)
    o_d = jnp.sum(mix_w[..., None].astype(vdh.dtype) * jnp.stack(outs, axis=0), axis=0)
    groups = jnp.concatenate([o_a.transpose(0, 2, 1, 3), o_b, o_c.transpose(0, 2, 1, 3),
                              o_d.transpose(0, 2, 1, 3)], axis=2)
    groups = rms_norm(groups, g_out.reshape(N_GROUPS, HEAD_DIM)).reshape(b, s, MIX_WIDTH)
    x = x + groups @ w_out
    h2 = rms_norm(x, g_ffn)
    return x + (jax.nn.silu(h2 @ w_gate) * (h2 @ w_up)) @ w_down

def first_inputs(seed: int = 0) -> dict:
    key = jax.random.key(seed)
    ks = jax.random.split(key, 23)
    L = DEPTH
    hd = HEAD_DIM

    def nrm(k, shape, scale):
        return jax.random.normal(k, shape, jnp.float32) * scale

    def gain(k, shape):
        return 1.0 + 0.02 * jax.random.normal(k, shape, jnp.float32)

    return {
        'x': nrm(ks[0], (BATCH, SEQ, D_MODEL), 1.0),
        'g_mix': gain(ks[1], (L, D_MODEL)),
        'w_in': nrm(ks[2], (L, D_MODEL, IN_COLS), D_MODEL ** -0.5),
        'b_gate': nrm(ks[3], (L, N_NSA_BRANCH * N_HEADS_A), 0.1),
        'g_q_nsa': gain(ks[4], (L, hd)),
        'g_k_cmp': gain(ks[5], (L, hd)),
        'g_k_slc': gain(ks[6], (L, hd)),
        'g_k_win': gain(ks[7], (L, hd)),
        'pe_k_cmp': nrm(ks[8], (L, CMP_LEN, hd), 0.1),
        'pe_v_cmp': nrm(ks[9], (L, CMP_LEN, hd), 0.1),
        'w1_k_cmp': nrm(ks[10], (L, CMP_LEN * hd, CMP_HIDDEN), (CMP_LEN * hd) ** -0.5),
        'w2_k_cmp': nrm(ks[11], (L, CMP_HIDDEN, hd), CMP_HIDDEN ** -0.5),
        'w1_v_cmp': nrm(ks[12], (L, CMP_LEN * hd, CMP_HIDDEN), (CMP_LEN * hd) ** -0.5),
        'w2_v_cmp': nrm(ks[13], (L, CMP_HIDDEN, hd), CMP_HIDDEN ** -0.5),
        'conv_w': nrm(ks[14], (L, CONV_K, CONV_CH), CONV_K ** -0.5),
        'g_q_dil': gain(ks[15], (L, hd)),
        'g_k_dil': gain(ks[16], (L, hd)),
        'g_out': gain(ks[17], (L, MIX_WIDTH)),
        'w_out': nrm(ks[18], (L, MIX_WIDTH, D_MODEL), MIX_WIDTH ** -0.5),
        'g_ffn': gain(ks[19], (L, D_MODEL)),
        'w_gate': nrm(ks[20], (L, D_MODEL, D_FF), D_MODEL ** -0.5),
        'w_up': nrm(ks[21], (L, D_MODEL, D_FF), D_MODEL ** -0.5),
        'w_down': nrm(ks[22], (L, D_FF, D_MODEL), D_FF ** -0.5),
    }

def first_block(x, g_mix, w_in, b_gate, g_q_nsa, g_k_cmp, g_k_slc, g_k_win, pe_k_cmp, pe_v_cmp,
              w1_k_cmp, w2_k_cmp, w1_v_cmp, w2_v_cmp, conv_w, g_q_dil, g_k_dil, g_out, w_out,
              g_ffn, w_gate, w_up, w_down):
    for l in range(DEPTH):
        x = hybrid_layer(x, g_mix[l], w_in[l], b_gate[l], g_q_nsa[l], g_k_cmp[l], g_k_slc[l], g_k_win[l],
                         pe_k_cmp[l], pe_v_cmp[l], w1_k_cmp[l], w2_k_cmp[l], w1_v_cmp[l], w2_v_cmp[l],
                         conv_w[l], g_q_dil[l], g_k_dil[l], g_out[l], w_out[l], g_ffn[l],
                         w_gate[l], w_up[l], w_down[l])
    return x


D_SSM = 512
SSM_GROUP = 16
N_SSM_GROUPS = D_SSM // SSM_GROUP
SSM_STATE = 64
D_ATTN = D_MODEL - D_SSM
N_Q_HEADS = D_ATTN // HEAD_DIM
N_KV_HEADS = 2
Q_PER_KV = N_Q_HEADS // N_KV_HEADS
KV_DIM = N_KV_HEADS * HEAD_DIM
D_IN = D_SSM + D_ATTN + 2 * KV_DIM
WINDOW = 128
N_BUCKETS = 32
MAX_DISTANCE = 128
D_FF_2 = 2816
CONV_WIDTH = 3
N_MOD = 6
EPS = 1e-6
NEG_INF_2 = -1e30


def _rms(x, w):
    xf = x.astype(jnp.float32)
    y = xf * lax.rsqrt(jnp.mean(xf * xf, axis=-1, keepdims=True) + EPS)
    return (y * w.astype(jnp.float32)).astype(x.dtype)

def _t5_bucket(n):
    n = np.maximum(n, 0)
    max_exact = N_BUCKETS // 2
    log_part = np.log(np.maximum(n, 1) / max_exact) / math.log(MAX_DISTANCE / max_exact)
    large = max_exact + (log_part * (N_BUCKETS - max_exact)).astype(np.int32)
    large = np.minimum(large, N_BUCKETS - 1)
    return np.where(n < max_exact, n, large).astype(np.int32)

def _s5(u, lam_re, lam_im, log_dt, b_re, b_im, c_re, c_im, d_skip, w_glu, b_glu):
    bsz, seq = u.shape[0], u.shape[1]
    f32 = jnp.float32
    ug = u.astype(f32).reshape(bsz, seq, N_SSM_GROUPS, SSM_GROUP)
    lr = jnp.minimum(lam_re.astype(f32), -1e-4)
    li = lam_im.astype(f32)
    dt = jnp.exp(log_dt.astype(f32))[:, None]
    mag = jnp.exp(dt * lr)
    a_re = mag * jnp.cos(dt * li)
    a_im = mag * jnp.sin(dt * li)
    den = lr * lr + li * li
    f_re = ((a_re - 1.0) * lr + a_im * li) / den
    f_im = (a_im * lr - (a_re - 1.0) * li) / den
    br = b_re.astype(f32)
    bi = b_im.astype(f32)
    bb_re = f_re[..., None] * br - f_im[..., None] * bi
    bb_im = f_re[..., None] * bi + f_im[..., None] * br
    bu_re = jnp.einsum("blgh,gph->blgp", ug, bb_re)
    bu_im = jnp.einsum("blgh,gph->blgp", ug, bb_im)
    shape_a = (1, seq, N_SSM_GROUPS, SSM_STATE)
    a_re_t = jnp.broadcast_to(a_re, shape_a)
    a_im_t = jnp.broadcast_to(a_im, shape_a)

    def combine(e1, e2):
        a1r, a1i, b1r, b1i = e1
        a2r, a2i, b2r, b2i = e2
        return (a2r * a1r - a2i * a1i,
                a2r * a1i + a2i * a1r,
                a2r * b1r - a2i * b1i + b2r,
                a2r * b1i + a2i * b1r + b2i)

    _, _, s_re, s_im = lax.associative_scan(combine, (a_re_t, a_im_t, bu_re, bu_im), axis=1)
    y = (jnp.einsum("blgp,ghp->blgh", s_re, c_re.astype(f32))
         - jnp.einsum("blgp,ghp->blgh", s_im, c_im.astype(f32))
         + d_skip.astype(f32).reshape(N_SSM_GROUPS, SSM_GROUP) * ug)
    z = jax.nn.gelu(y.reshape(bsz, seq, D_SSM))
    out = z * jax.nn.sigmoid(z @ w_glu.astype(f32) + b_glu.astype(f32))
    return out.astype(u.dtype)

def _swa_sink(q, k, v, rel_bias, sinks):
    bsz, seq = q.shape[0], q.shape[1]
    nb = seq // BLOCK
    f32 = jnp.float32
    qb = q.astype(f32).reshape(bsz, nb, BLOCK, N_KV_HEADS, Q_PER_KV, HEAD_DIM)
    pad = ((0, 0), (BLOCK, 0), (0, 0), (0, 0))
    kb = jnp.pad(k.astype(f32), pad).reshape(bsz, nb + 1, BLOCK, N_KV_HEADS, HEAD_DIM)
    vb = jnp.pad(v.astype(f32), pad).reshape(bsz, nb + 1, BLOCK, N_KV_HEADS, HEAD_DIM)
    k_band = jnp.concatenate([kb[:, :-1], kb[:, 1:]], axis=2)
    v_band = jnp.concatenate([vb[:, :-1], vb[:, 1:]], axis=2)
    logits = jnp.einsum("bnqhgd,bnkhd->bnhgqk", qb, k_band) * (HEAD_DIM ** -0.5)
    q_off = np.arange(BLOCK)[:, None] + BLOCK
    k_off = np.arange(2 * BLOCK)[None, :]
    dist = q_off - k_off
    bias = jnp.take(rel_bias.astype(f32), _t5_bucket(dist), axis=0)
    bias = bias.transpose(2, 0, 1).reshape(N_KV_HEADS, Q_PER_KV, BLOCK, 2 * BLOCK)
    key_pos = np.arange(nb)[:, None, None] * BLOCK + k_off[None] - BLOCK
    mask = (dist[None] >= 0) & (dist[None] < WINDOW) & (key_pos >= 0)
    logits = jnp.where(mask[None, :, None, None], logits + bias, NEG_INF_2)
    sink = sinks.astype(f32).reshape(N_KV_HEADS, Q_PER_KV)[None, None, :, :, None, None]
    m = jnp.maximum(jnp.max(logits, axis=-1, keepdims=True), sink)
    p = jnp.exp(logits - m)
    probs = p / (jnp.sum(p, axis=-1, keepdims=True) + jnp.exp(sink - m))
    out = jnp.einsum("bnhgqk,bnkhd->bnqhgd", probs, v_band)
    return out.reshape(bsz, seq, D_ATTN).astype(q.dtype)

def _conv_ffn(h, w_up, conv_w, conv_b, w_down):
    up = h @ w_up
    rhs = conv_w.reshape(CONV_WIDTH, 1, 2 * D_FF_2).astype(up.dtype)
    up = lax.conv_general_dilated(up, rhs, window_strides=(1,),
                                  padding=[(CONV_WIDTH - 1, 0)],
                                  dimension_numbers=("NWC", "WIO", "NWC"),
                                  feature_group_count=2 * D_FF_2) + conv_b
    val, gate = jnp.split(up, 2, axis=-1)
    return (jax.nn.silu(gate) * val) @ w_down

def second_inputs(seed: int = 0) -> dict:
    key = jax.random.key(seed)
    ks = jax.random.split(key, 28)
    f32 = jnp.float32

    def nrm(k, shape, scale):
        return jax.random.normal(k, shape, f32) * scale

    def gain(k, shape):
        return 1.0 + 0.05 * jax.random.normal(k, shape, f32)

    G, P, H = N_SSM_GROUPS, SSM_STATE, SSM_GROUP
    lam_im0 = math.pi * jnp.arange(P, dtype=f32)
    return {
        "x": nrm(ks[0], (BATCH, SEQ, D_MODEL), 1.0),
        "c": nrm(ks[1], (BATCH, D_MODEL), 1.0),
        "w_mod": nrm(ks[2], (DEPTH, D_MODEL, N_MOD * D_MODEL), 0.5 * D_MODEL ** -0.5),
        "b_mod": nrm(ks[3], (DEPTH, N_MOD * D_MODEL), 0.02),
        "norm1_w": gain(ks[4], (DEPTH, D_MODEL)),
        "w_in": nrm(ks[5], (DEPTH, D_MODEL, D_IN), D_MODEL ** -0.5),
        "lam_re": -0.5 * jnp.exp(0.1 * jax.random.normal(ks[6], (DEPTH, G, P), f32)),
        "lam_im": lam_im0 + 0.05 * jax.random.normal(ks[7], (DEPTH, G, P), f32),
        "log_dt": jax.random.uniform(ks[8], (DEPTH, G), f32, math.log(1e-3), math.log(1e-1)),
        "ssm_b_re": nrm(ks[9], (DEPTH, G, P, H), (2 * H) ** -0.5),
        "ssm_b_im": nrm(ks[10], (DEPTH, G, P, H), (2 * H) ** -0.5),
        "ssm_c_re": nrm(ks[11], (DEPTH, G, H, P), (2 * P) ** -0.5),
        "ssm_c_im": nrm(ks[12], (DEPTH, G, H, P), (2 * P) ** -0.5),
        "ssm_d": nrm(ks[13], (DEPTH, D_SSM), 1.0),
        "w_glu": nrm(ks[14], (DEPTH, D_SSM, D_SSM), D_SSM ** -0.5),
        "b_glu": nrm(ks[15], (DEPTH, D_SSM), 0.02),
        "q_norm_w": gain(ks[16], (DEPTH, HEAD_DIM)),
        "k_norm_w": gain(ks[17], (DEPTH, HEAD_DIM)),
        "rel_bias": nrm(ks[18], (N_BUCKETS, N_Q_HEADS), 0.5),
        "sinks": nrm(ks[19], (DEPTH, N_Q_HEADS), 0.5),
        "out_norm_ssm": gain(ks[20], (DEPTH, D_SSM)),
        "out_norm_attn": gain(ks[21], (DEPTH, D_ATTN)),
        "w_out": nrm(ks[22], (DEPTH, D_MODEL, D_MODEL), D_MODEL ** -0.5),
        "norm2_w": gain(ks[23], (DEPTH, D_MODEL)),
        "w_up": nrm(ks[24], (DEPTH, D_MODEL, 2 * D_FF_2), D_MODEL ** -0.5),
        "conv_w": nrm(ks[25], (DEPTH, CONV_WIDTH, 2 * D_FF_2), CONV_WIDTH ** -0.5),
        "conv_b": nrm(ks[26], (DEPTH, 2 * D_FF_2), 0.02),
        "w_down": nrm(ks[27], (DEPTH, D_FF_2, D_MODEL), D_FF_2 ** -0.5),
    }

def second_block(x, c, w_mod, b_mod, norm1_w, w_in, lam_re, lam_im, log_dt,
              ssm_b_re, ssm_b_im, ssm_c_re, ssm_c_im, ssm_d, w_glu, b_glu,
              q_norm_w, k_norm_w, rel_bias, sinks, out_norm_ssm, out_norm_attn,
              w_out, norm2_w, w_up, conv_w, conv_b, w_down):
    bsz, seq = x.shape[0], x.shape[1]
    c_act = jax.nn.silu(c)
    for l in range(DEPTH):
        mod = (c_act @ w_mod[l] + b_mod[l])[:, None, :]
        sh1, sc1, g1, sh2, sc2, g2 = jnp.split(mod, N_MOD, axis=-1)

        h = _rms(x, norm1_w[l]) * (1 + sc1) + sh1
        proj = h @ w_in[l]
        u, q, k, v = jnp.split(proj, [D_SSM, D_SSM + D_ATTN, D_SSM + D_ATTN + KV_DIM], axis=-1)
        y_ssm = _s5(u, lam_re[l], lam_im[l], log_dt[l], ssm_b_re[l], ssm_b_im[l],
                    ssm_c_re[l], ssm_c_im[l], ssm_d[l], w_glu[l], b_glu[l])
        q = _rms(q.reshape(bsz, seq, N_Q_HEADS, HEAD_DIM), q_norm_w[l])
        k = _rms(k.reshape(bsz, seq, N_KV_HEADS, HEAD_DIM), k_norm_w[l])
        v = v.reshape(bsz, seq, N_KV_HEADS, HEAD_DIM)
        y_attn = _swa_sink(q, k, v, rel_bias, sinks[l])
        mixed = jnp.concatenate([_rms(y_ssm, out_norm_ssm[l]),
                                 _rms(y_attn, out_norm_attn[l])], axis=-1)
        x = x + g1 * (mixed @ w_out[l])

        h2 = _rms(x, norm2_w[l]) * (1 + sc2) + sh2
        x = x + g2 * _conv_ffn(h2, w_up[l], conv_w[l], conv_b[l], w_down[l])
    return x


def setup_inputs(seed=0):
    out = dict(first_inputs(seed))
    for name, value in second_inputs(seed + 1).items():
        if name != "x":
            out[name + "_2"] = value
    return out


def reference(
    x, g_mix, w_in, b_gate, g_q_nsa, g_k_cmp, g_k_slc, g_k_win, pe_k_cmp, pe_v_cmp, w1_k_cmp,
    w2_k_cmp, w1_v_cmp, w2_v_cmp, conv_w, g_q_dil, g_k_dil, g_out, w_out, g_ffn, w_gate, w_up,
    w_down, c_2, w_mod_2, b_mod_2, norm1_w_2, w_in_2, lam_re_2, lam_im_2, log_dt_2, ssm_b_re_2,
    ssm_b_im_2, ssm_c_re_2, ssm_c_im_2, ssm_d_2, w_glu_2, b_glu_2, q_norm_w_2, k_norm_w_2,
    rel_bias_2, sinks_2, out_norm_ssm_2, out_norm_attn_2, w_out_2, norm2_w_2, w_up_2, conv_w_2,
    conv_b_2, w_down_2,
):
    x = first_block(
        x, g_mix, w_in, b_gate, g_q_nsa, g_k_cmp, g_k_slc, g_k_win, pe_k_cmp, pe_v_cmp,
        w1_k_cmp, w2_k_cmp, w1_v_cmp, w2_v_cmp, conv_w, g_q_dil, g_k_dil, g_out, w_out, g_ffn,
        w_gate, w_up, w_down,
    )
    return second_block(
        x, c_2, w_mod_2, b_mod_2, norm1_w_2, w_in_2, lam_re_2, lam_im_2, log_dt_2, ssm_b_re_2,
        ssm_b_im_2, ssm_c_re_2, ssm_c_im_2, ssm_d_2, w_glu_2, b_glu_2, q_norm_w_2, k_norm_w_2,
        rel_bias_2, sinks_2, out_norm_ssm_2, out_norm_attn_2, w_out_2, norm2_w_2, w_up_2,
        conv_w_2, conv_b_2, w_down_2,
    )


_drawn_inputs = setup_inputs


def setup_inputs(seed=0):
    import zlib

    import numpy as np

    out = dict(_drawn_inputs(seed))
    spreads = {}
    factors = {'b_gate': 2.833,
     'g_q_nsa': 8.0,
     'g_k_cmp': 8.0,
     'g_k_slc': 8.0,
     'g_k_win': 8.0,
     'pe_k_cmp': 6.826,
     'g_q_dil': 8.0,
     'g_k_dil': 7.6,
     'g_out': 3.765,
     'g_ffn': 5.037,
     'b_mod_2': 2.922,
     'norm1_w_2': 6.017,
     'lam_re_2': 64.0,
     'lam_im_2': 46.488,
     'log_dt_2': 55.248,
     'ssm_b_re_2': 64.0,
     'ssm_b_im_2': 64.0,
     'ssm_c_re_2': 64.0,
     'ssm_c_im_2': 59.232,
     'b_glu_2': 64.0,
     'q_norm_w_2': 8.0,
     'k_norm_w_2': 8.0,
     'sinks_2': 188.538,
     'out_norm_ssm_2': 63.76,
     'out_norm_attn_2': 63.328,
     'norm2_w_2': 16.169,
     'conv_b_2': 30.72,
     'rel_bias_2': 8.0}
    for name, (base, spread) in spreads.items():
        noise = np.random.default_rng([zlib.crc32(name.encode()), seed]).standard_normal(out[name].shape)
        drawn = base * np.exp(spread * noise) if base else spread * noise
        out[name] = jnp.asarray(drawn.astype(out[name].dtype))
    for name, factor in factors.items():
        out[name] = (out[name] * factor).astype(out[name].dtype)
    return out
```

```python
from contextlib import ExitStack

import numpy as np

import concourse.bass as bass
from concourse import mybir

F = mybir.dt.float32
R = mybir.dt.float32r
ACT = mybir.ActivationFunctionType
ALU = mybir.AluOpType
AX = mybir.AxisListType

P = 128
S = 512
D = 1024
KT = D // P
NT = S // P
HD = 64
CW = 2048
FF = 2816
FT = FF // P
HALF = FT // 2
NCMP = (S - 32) // 16 + 1
NEG = -1e30
EPS = 1e-6
LAG = 2
TWO_PI = 6.283185307179586
ROUND = 12582912.0

T_QA, T_CV, T_KSW, T_CB, T_CC, T_CU, T_QC, T_KC, T_QD, T_KD = 0, 2, 3, 4, 6, 8, 10, 12, 14, 16
NORMED = (0, 1, 3, 14, 15, 16, 17)


class Core:
    pass


class RmsSignals:
    def __init__(self, squared, summed, rooted, scaled, rounded, split):
        self.squared, self.summed, self.rooted = squared, summed, rooted
        self.scaled, self.rounded, self.split = scaled, rounded, split


class Unit:

    def __init__(self, branch, i, q, key, width, blocks, table, gate=None, sink=None, nsink=None):
        self.branch, self.i, self.q, self.key, self.width, self.blocks = branch, i, q, key, width, blocks
        self.table, self.gate, self.sink, self.nsink = table, gate, sink, nsink


class Branch:

    def __init__(self, group, products, out, first=True, stop=True, extra=None):
        self.group, self.products, self.out = group, products, out
        self.first, self.stop, self.extra = first, stop, extra


class Own:

    def __init__(self, dve_sem):
        self.dve, self.act, self.pool, self.dve_sem = 0, 0, 0, dve_sem


def layout(parts):
    at, out = 0, {}
    for name, width in parts:
        out[name] = (at, at + width)
        at += width
    return out, at


KEPT, NKEPT = layout([("ident", P), ("ind", 8 * 16)])
CONST, NCONST = layout([("negtri", P), ("past", P), ("future", P), ("dist", S), ("causal", S), ("dilated", S),
                        ("cdist", NT * NCMP), ("cmask", NT * NCMP), ("cvis", NT * NCMP)])
PARAM, NPARAM = layout([("g_mix", 8), ("g_ffn", 8), ("g_heads", 7), ("g_kcmp", 1), ("g_out", 8), ("conv", 6),
                        ("pe", 32), ("b_gate", 48), ("w2k", 256), ("w2v", 128),
                        ("c", 8), ("b_mod", 48), ("norm1", 8), ("norm2", 8), ("lam_re", 16), ("lam_im", 16),
                        ("log_dt", 16), ("d_skip", 4), ("b_glu", 4), ("g_heads2", 5), ("sinks", 8),
                        ("o_ssm", 4), ("o_attn", 4), ("convw2", 132), ("convb2", 44)])


class Chain:

    def __init__(self, eng, sem, start=0):
        self.eng, self.sem, self.n = eng, sem, start

    def link(self, ins):
        self.n += 1
        ins.then_inc(self.sem, 1)
        self.eng.wait_ge(self.sem, self.n)

    def mark(self, ins):
        self.n += 1
        ins.then_inc(self.sem, 1)
        return self.n

    def need(self, n):
        self.eng.wait_ge(self.sem, n)



def load_chunk(eng, k, slot, src, after_lo=None):
    if after_lo is not None:
        eng.wait_ge(k.w_lo, after_lo)
    width = src.shape[-1]
    eng.dma_start(k.raw[:, slot, 0:width], src).then_inc(k.w_loaded[slot], 16)


def round_chunk(act, k, slot, loaded, used, width=CW):
    act.wait_ge(k.w_loaded[slot], loaded)
    if used is not None:
        act.wait_ge(k.w_used, used)
    act.activation(k.whi[:, slot, 0:width], k.raw[:, slot, 0:width], ACT.Copy).then_inc(k.w_hi, 1)


def rest_chunk(dve, k, slot, hi, width=CW):
    dve.wait_ge(k.w_hi, hi)
    dve.tensor_tensor(k.wlo[:, slot, 0:width], k.raw[:, slot, 0:width], k.whi[:, slot, 0:width].bitcast(F),
                      ALU.subtract).then_inc(k.w_lo, 1)


def split_mm(pe, out, whi, wlo, xhi, xlo, first, last):
    pe.matmul(out, whi, xhi, start=first, stop=False)
    pe.matmul(out, whi, xlo, start=False, stop=False)
    return pe.matmul(out, wlo, xhi, start=False, stop=last)


def pe_tiles(pe, k, slot, banks, xhi, xlo):
    hi = k.whi[:, slot, :].rearrange("p (k n) -> p k n", n=256)
    lo = k.wlo[:, slot, :].rearrange("p (k n) -> p k n", n=256)
    for t in range(2):
        cols = slice(P * t, P * t + P)
        for j in range(KT):
            mm = split_mm(pe, banks[t], hi[:, j, cols], lo[:, j, cols], xhi[:, j, :], xlo[:, j, :],
                          j == 0, j == KT - 1)
    return mm


def pe_tokens(pe, k, slot, width, outs, xhi, xlo):
    hi = k.whi[:, slot, 0:KT * width].rearrange("p (k n) -> p k n", n=width)
    lo = k.wlo[:, slot, 0:KT * width].rearrange("p (k n) -> p k n", n=width)
    for i in range(NT):
        tok = slice(P * i, P * i + P)
        for j in range(KT):
            mm = split_mm(pe, outs[i], xhi[:, j, tok], xlo[:, j, tok], hi[:, j, :], lo[:, j, :],
                          j == 0, j == KT - 1)
    return mm



def rms_signals(k, name):
    return RmsSignals(*(k.sem(f"{name}_{what}") for what in
                        ("squared", "summed", "rooted", "scaled", "rounded", "split")))


def rms_act(act, k, src, n, sig, hi, eps_col):
    for j in range(n):
        if j >= 4:
            act.wait_ge(sig.summed, j - 3)
        act.activation(k.sq[:, j % 4, :], src(j), ACT.Square).then_inc(sig.squared, 1)
    act.wait_ge(sig.summed, n)
    act.activation(k.root[:, :], k.bank[0][:, :], ACT.Sqrt, bias=eps_col, scale=1.0 / (P * n)).then_inc(sig.rooted, 1)
    for j in range(n):
        act.wait_ge(sig.scaled, j + 1)
        act.activation(hi(j), k.sq[:, j % 4, :], ACT.Copy).then_inc(sig.rounded, 1)


def rms_pe(pe, k, n, sig):
    for j in range(n):
        pe.wait_ge(sig.squared, j + 1)
        pe.matmul(k.bank[0][:, :], k.ones[:, :], k.sq[:, j % 4, :], start=(j == 0),
                  stop=(j == n - 1)).then_inc(sig.summed, 1)


def rms_dve(dve, k, src, n, sig, gain, shift, lo, hi, chain):
    dve.wait_ge(sig.rooted, 1)
    chain.link(dve.reciprocal(k.root[:, :], k.root[:, :]))

    def scale(j):
        if j >= 4:
            dve.wait_ge(sig.split, j - 3)
        ins = dve.scalar_tensor_tensor(out=k.sq[:, j % 4, :], in0=src(j), scalar=gain(j), in1=k.root[:, :],
                                       op0=ALU.mult, op1=ALU.mult)
        if shift is not None:
            chain.link(ins)
            ins = dve.tensor_scalar(k.sq[:, j % 4, :], k.sq[:, j % 4, :], shift(j), None, ALU.add)
        ins.then_inc(sig.scaled, 1)

    for j in range(min(n, 3)):
        scale(j)
    for j in range(n):
        if j + 3 < n:
            scale(j + 3)
        dve.wait_ge(sig.rounded, j + 1)
        dve.tensor_tensor(lo(j), k.sq[:, j % 4, :], hi(j).bitcast(F), ALU.subtract).then_inc(sig.split, 1)



def hidden_stage(nc, k, name, x, xhi, xlo, hhi, hlo, norm, base, w_two, w_down, taps, own):
    sig, gain, shift, eps_col = norm
    free, made, rounded, split, silued, conved, made_taps = (k.sem(f"{name}_{w}") for w in (
        "banks_free", "made", "rounded", "split", "silu", "convolved", "middle_tap"))
    pairs = FT // 2

    def tile(t, i, s):
        return t[:, bass.ds(2 * i + s, 1), :].rearrange("p a t -> p (a t)")

    with nc.Block() as block:

        @block.sync
        def _(sp):
            by_slot = w_two.rearrange("(i s) p c -> s i p c", s=2)
            with sp.Fori(2, pairs) as i:
                for s in range(2):
                    sp.wait_ge(k.w_lo, 2 * i + (base + s - 1))
                    sp.dma_start(k.raw[:, s, :], by_slot[s][bass.ds(i, 1), :, :].rearrange("i p c -> p (i c)"))\
                        .then_inc(k.w_loaded[s], 16)
            for n in range(4):
                load_chunk(sp, k, n % 2, w_down[n], after_lo=base + FT + n - 1)

        @block.scalar
        def _(act):
            rms_act(act, k, lambda j: x[:, j, :], KT, sig, lambda j: xhi[:, j, :], eps_col)
            with act.Fori(0, pairs) as i:
                for s in range(2):
                    round_chunk(act, k, s, 16 * i + 16 * (base // 2 + 2), 2 * i + (base + s + 1))
                    if taps is None:
                        act.activation(k.sq[:, 2 * s + 1, :], k.bank[2 * s][:, :], ACT.Silu).then_inc(silued, 1)
                        act.wait_ge(free, 2 * i + (s + 3))
                    else:
                        for a in range(2):
                            act.activation(k.sq[:, 2 * s + a, :], k.bank[2 * s + a][:, :], ACT.Identity,
                                           bias=taps[1][:, bass.ds(4 * i + (2 * s + a), 1)],
                                           scale=taps[0][:, bass.ds(12 * i + (6 * s + 3 * a + 2), 1)])\
                                .then_inc(conved, 1)
                        act.wait_ge(free, 2 * i + (s + 3))
                        act.activation(k.sq[:, 2 * s + 1, :], k.sq[:, 2 * s + 1, :], ACT.Silu).then_inc(silued, 1)
                        act.wait_ge(made, 2 * i + (s + 1))
                    act.activation(tile(hhi, i, s), k.sq[:, 2 * s, :], ACT.Copy).then_inc(rounded, 1)

        @block.vector
        def _(dve):
            chain = Chain(dve, own.dve_sem, own.dve)
            rms_dve(dve, k, lambda j: x[:, j, :], KT, sig, gain, shift, lambda j: xlo[:, j, :],
                    lambda j: xhi[:, j, :], chain)
            own.dve = chain.n
            dve.sem_inc(free, 2)
            with dve.Fori(0, pairs) as i:
                for s in range(2):
                    rest_chunk(dve, k, s, 2 * i + (base + s + 3))
                    if taps is None:
                        dve.wait_ge(silued, 2 * i + (s + 1))
                        dve.tensor_tensor(k.sq[:, 2 * s, :], k.sq[:, 2 * s + 1, :], k.bank[2 * s + 1][:, :],
                                          ALU.mult).then_inc(free, 1)
                    else:
                        for a in range(2):
                            dve.wait_ge(conved, 4 * i + (2 * s + a + 1))
                            for back in (1, 2):
                                y = k.sq[:, 2 * s + a, back:S]
                                ins = dve.scalar_tensor_tensor(
                                    out=y, in0=k.bank[2 * s + a][:, 0:S - back],
                                    scalar=taps[0][:, bass.ds(12 * i + (6 * s + 3 * a + 2 - back), 1)], in1=y,
                                    op0=ALU.mult, op1=ALU.add)
                                if back == 1:
                                    ins.then_inc(made_taps, 1)
                                    dve.wait_ge(made_taps, 4 * i + (2 * s + a + 1))
                        ins.then_inc(free, 1)
                        dve.wait_ge(silued, 2 * i + (s + 1))
                        dve.tensor_tensor(k.sq[:, 2 * s, :], k.sq[:, 2 * s, :], k.sq[:, 2 * s + 1, :],
                                          ALU.mult).then_inc(made, 1)
                    dve.wait_ge(rounded, 2 * i + (s + 1))
                    dve.tensor_tensor(tile(hlo, i, s), k.sq[:, 2 * s, :], tile(hhi, i, s).bitcast(F),
                                      ALU.subtract).then_inc(split, 1)

        @block.tensor
        def _(pe):
            rms_pe(pe, k, KT, sig)
            pe.wait_ge(sig.split, KT)
            with pe.Fori(0, pairs) as i:
                for s in range(2):
                    pe.wait_ge(k.w_lo, 2 * i + (base + s + 1))
                    pe.wait_ge(free, 2 * i + (s + 1))
                    pe_tiles(pe, k, s, [k.bank[2 * s][:, :], k.bank[2 * s + 1][:, :]], xhi, xlo).then_inc(k.w_used, 1)


def down_stage(nc, k, name, x, hhi, hlo, base, w_down, following, gain, mod, store):
    added, stored = k.sem(f"{name}_added"), k.sem(f"{name}_stored")
    quads = KT // 2
    halves = HALF * P

    with nc.Block() as block:

        @block.sync
        def _(sp):
            by_turn = w_down.rearrange("(i q) p c -> q i p c", q=4)

            def load(i, q):
                sp.wait_ge(k.w_lo, 4 * i + (base + q - 1))
                sp.dma_start(k.raw[:, q % 2, 0:halves], by_turn[q][bass.ds(i, 1), :, :].rearrange("i p c -> p (i c)"))\
                    .then_inc(k.w_loaded[q % 2], 16)

            if mod is not None:
                for q in range(4):
                    mod.load_first(sp, q)
            with sp.Fori(1, quads) as i:
                for q in range(4):
                    load(i, q)
                    if mod is not None:
                        mod.load(sp, i, q)
            if following is not None:
                for n in range(4):
                    load_chunk(sp, k, n % 2, following[n], after_lo=base + 2 * KT + n - 1)
            if store is not None:
                for j in range(KT):
                    sp.wait_ge(added, j + 1)
                    sp.dma_start(store[:, j, :], x[:, j, :]).then_inc(stored, 16)
                sp.wait_ge(stored, 16 * KT)

        @block.scalar
        def _(act):
            def split(i, q, width=CW):
                round_chunk(act, k, q % 2, 32 * i + 16 * ((base + q) // 2 + 2), 4 * i + (base + q + 1), width)

            if mod is not None:
                mod.start(act)
            with act.Fori(0, quads - 1) as i:
                for q in range(4):
                    split(i, q, halves)
            for q in range(4 if following is not None else 2):
                split(quads - 1, q, CW if q >= 2 else halves)

        @block.vector
        def _(dve):
            def turn(i, q, width):
                if mod is not None:
                    mod.multiply(dve, i, q)
                if width:
                    rest_chunk(dve, k, q % 2, 4 * i + (base + q + 3), width)
                if q % 2:
                    dve.wait_ge(k.w_used, 4 * i + (base + q + 1))
                    t = q // 2
                    xt = x[:, bass.ds(2 * i + t, 1), :].rearrange("p a t -> p (a t)")
                    if gain is None:
                        ins = dve.tensor_tensor(xt, xt, k.bank[t][:, :], ALU.add)
                    else:
                        ins = dve.scalar_tensor_tensor(out=xt, in0=k.bank[t][:, :],
                                                       scalar=gain[:, bass.ds(2 * i + t, 1)], in1=xt,
                                                       op0=ALU.mult, op1=ALU.add)
                    ins.then_inc(added, 1)

            for q in range(4):
                turn(0, q, halves)
            with dve.Fori(1, quads - 1) as i:
                for q in range(4):
                    turn(i, q, halves)
            for q in range(4):
                turn(quads - 1, q, halves if q < 2 else (CW if following is not None else 0))
            if mod is not None:
                mod.finish(dve)

        @block.tensor
        def _(pe):
            def turn(i, t, wait):
                if wait:
                    pe.wait_ge(added, 2 * i + (t - 1))
                for s in range(2):
                    q = 2 * t + s
                    pe.wait_ge(k.w_lo, 4 * i + (base + q + 1))
                    hi = k.whi[:, s, 0:halves].rearrange("p (k n) -> p k n", n=P)
                    lo = k.wlo[:, s, 0:halves].rearrange("p (k n) -> p k n", n=P)
                    for j in range(HALF):
                        mm = split_mm(pe, k.bank[t][:, :], hi[:, j, :], lo[:, j, :], hhi[:, HALF * s + j, :],
                                      hlo[:, HALF * s + j, :], q % 2 == 0 and j == 0, q % 2 == 1 and j == HALF - 1)
                    mm.then_inc(k.w_used, 1)
                    if mod is not None:
                        mod.reduce(pe, i, q)

            for t in range(2):
                turn(0, t, False)
            with pe.Fori(1, quads) as i:
                for t in range(2):
                    turn(i, t, True)



class Modulation:
    W = 384

    def __init__(self, k, io, sb, ctx, pr, mods):
        self.k, self.w, self.mods, self.pr = k, io["w_mod"], mods, pr
        self.slots = sb("mod_w", [P, 2, KT * self.W], ctx=ctx)
        self.acc = sb("mod_acc", [P, 2, self.W], ctx=ctx)
        self.c = sb("mod_c", [P, KT], ctx=ctx)
        self.ready, self.step, self.reduced = k.sem("mod_c_ready"), k.sem("mod_step"), k.sem("mod_reduced")
        self.loaded = [k.sem("mod_loaded0"), k.sem("mod_loaded1")]

    def load(self, sp, i, q):
        by_turn = self.w.rearrange("(i q) p c -> q i p c", q=4)
        sp.wait_ge(self.step, 32 * i + 8 * (q - 1))
        sp.dma_start(self.slots[:, q % 2, :], by_turn[q][bass.ds(i, 1), :, :].rearrange("i p c -> p (i c)"))\
            .then_inc(self.loaded[q % 2], 16)

    def load_first(self, sp, q):
        if q >= 2:
            sp.wait_ge(self.step, 8 * (q - 1))
        sp.dma_start(self.slots[:, q % 2, :], self.w[q]).then_inc(self.loaded[q % 2], 16)

    def start(self, act):
        act.activation(self.c[:, :], self.pr("c"), ACT.Silu).then_inc(self.ready, 1)

    def multiply(self, dve, i, q):
        dve.wait_ge(self.ready, 1)
        dve.wait_ge(self.loaded[q % 2], 32 * i + 16 * (q // 2 + 1))
        acc = self.acc[:, q % 2, :]
        for j in range(KT):
            w = self.slots[:, q % 2, self.W * j:self.W * j + self.W]
            if j == 0:
                if q >= 2:
                    dve.wait_ge(self.reduced, 4 * i + (q - 1))
                elif not isinstance(i, int) or i > 0:
                    dve.wait_ge(self.reduced, 4 * i + (q - 1))
                ins = dve.tensor_scalar(acc, w, self.c[:, 0:1], None, ALU.mult)
            else:
                dve.wait_ge(self.step, 32 * i + (8 * q + j))
                ins = dve.scalar_tensor_tensor(out=acc, in0=w, scalar=self.c[:, j:j + 1], in1=acc,
                                               op0=ALU.mult, op1=ALU.add)
            ins.then_inc(self.step, 1)

    def reduce(self, pe, i, q):
        pe.wait_ge(self.step, 32 * i + 8 * (q + 1))
        for t in range(3):
            mm = pe.matmul(self.k.bank[7][:, bass.ds(12 * i + (3 * q + t), 1)], self.acc[:, q % 2, P * t:P * t + P],
                           self.k.ones[:, 0:1], start=True, stop=True)
        mm.then_inc(self.reduced, 1)

    def finish(self, dve):
        dve.wait_ge(self.reduced, 16)
        dve.tensor_tensor(self.mods[:, :], self.k.bank[7][:, 0:48], self.pr("b_mod"), ALU.add).then_inc(self.step, 1)



def attention(k, name, units, branches, tables_ready):
    n = len(units)
    scored, biased, maxed, exped, normed, turned, moved, summed, stored = (
        k.sem(f"{name}_{w}") for w in ("scored", "biased", "maxed", "exped", "normed", "turned", "moved",
                                       "summed", "stored"))
    sbank = (k.bank[0], k.bank[1], k.bank[6])
    tbank = (k.bank[2], k.bank[3])
    obank = (k.bank[4], k.bank[5])
    groups = [b.group for b in branches]
    last_unit = {}
    for u, unit in enumerate(units):
        last_unit[unit.branch] = u

    def pe_part(pe):
        def scores(u):
            unit = units[u]
            if u >= 3:
                pe.wait_ge(biased, u - 2)
            pe.matmul(sbank[u % 3][:, 0:unit.width], unit.q, unit.key, start=True, stop=True).then_inc(scored, 1)

        def turn(u):
            unit = units[u]
            pe.wait_ge(normed, u + 1)
            if u >= 2:
                pe.wait_ge(moved, u - 1)
            for b in range(len(unit.blocks)):
                mm = pe.transpose(tbank[u % 2][:, P * b:P * b + P], k.prob[:, u % 4, P * b:P * b + P], k.ident)
            mm.then_inc(turned, 1)

        def values(b):
            br = branches[b]
            pe.wait_ge(moved, last_unit[b] + 1)
            if br.first and br.group >= 2:
                pe.wait_ge(stored, br.group - 1)
            out = obank[br.group % 2]
            if br.extra is not None:
                pe.matmul(out[0:HD, :], br.extra[0], br.extra[1], start=True, stop=True)
            for lhs, rhs, lo, hi, start in br.products(k.probT[:, b % 2]):
                mm = pe.matmul(out[0:HD, lo:hi], lhs, rhs, start=start, stop=True, skip_group_check=not start)
            mm.then_inc(summed, 1)

        for u in range(min(LAG, n)):
            scores(u)
        for u in range(n + 1):
            if u + LAG < n:
                scores(u + LAG)
            if u < n:
                turn(u)
            if u >= 1 and last_unit[units[u - 1].branch] == u - 1:
                values(units[u - 1].branch)

    def dve_part(dve, chain):
        def bias(u):
            unit = units[u]
            dve.wait_ge(scored, u + 1)
            if u >= 4:
                dve.wait_ge(turned, u - 3)
            dve.tensor_tensor_reduce(k.prob[:, u % 4, 0:unit.width], sbank[u % 3][:, 0:unit.width], unit.table, 1.0,
                                     NEG, ALU.add, ALU.max, k.nmax[:, u:u + 1]).then_inc(biased, 1)
            dve.wait_ge(biased, u + 1)
            if unit.sink is not None:
                ins = dve.scalar_tensor_tensor(out=k.nmax[:, u:u + 1], in0=k.nmax[:, u:u + 1], scalar=-1.0,
                                               in1=unit.nsink, op0=ALU.mult, op1=ALU.min)
            else:
                ins = dve.tensor_scalar(k.nmax[:, u:u + 1], k.nmax[:, u:u + 1], -1.0, None, ALU.mult)
            ins.then_inc(maxed, 1)

        def normalise(u):
            unit = units[u]
            dve.wait_ge(exped, u + 1)
            if unit.sink is not None:
                chain.link(dve.tensor_tensor(k.rsum[:, u:u + 1], k.rsum[:, u:u + 1], k.esink[:, u:u + 1], ALU.add))
            chain.link(dve.reciprocal(k.rsum[:, u:u + 1], k.rsum[:, u:u + 1]))
            if unit.gate is not None:
                dve.tensor_scalar(k.prob[:, u % 4, 0:unit.width], k.prob[:, u % 4, 0:unit.width],
                                  k.rsum[:, u:u + 1], unit.gate, ALU.mult, ALU.mult).then_inc(normed, 1)
            else:
                dve.tensor_scalar(k.prob[:, u % 4, 0:unit.width], k.prob[:, u % 4, 0:unit.width],
                                  k.rsum[:, u:u + 1], None, ALU.mult).then_inc(normed, 1)

        for u in range(n + 1):
            if u < n:
                bias(u)
            if u >= 1:
                normalise(u - 1)

    def act_part(act):
        def exps(u):
            unit = units[u]
            act.wait_ge(maxed, u + 1)
            if unit.sink is not None:
                act.activation(k.esink[:, u:u + 1], unit.sink, ACT.Exp, bias=k.nmax[:, u:u + 1])
            act.activation(k.prob[:, u % 4, 0:unit.width], k.prob[:, u % 4, 0:unit.width], ACT.Exp,
                           bias=k.nmax[:, u:u + 1], accum_out=k.rsum[:, u:u + 1]).then_inc(exped, 1)

        def move(u):
            unit = units[u]
            b = unit.branch
            act.wait_ge(turned, u + 1)
            if b >= 2:
                act.wait_ge(summed, b - 1)
            w = P * len(unit.blocks)
            act.activation(k.probT[:, b % 2, unit.blocks[0]:unit.blocks[-1] + 1, P * unit.i:P * unit.i + P],
                           tbank[u % 2][:, 0:w].rearrange("p (b q) -> p b q", q=P), ACT.Copy).then_inc(moved, 1)

        def store(b):
            g = groups[b]
            act.wait_ge(summed, b + 1)
            act.activation(branches[b].out, obank[g % 2][0:HD, :], ACT.Copy).then_inc(stored, 1)

        for u in range(n + 5):
            if u < n:
                exps(u)
            if 2 <= u < n + 2:
                move(u - 2)
            if u >= 4 and u - 4 < n:
                b = units[u - 4].branch
                if last_unit[b] == u - 4 and branches[b].stop:
                    store(b)

    return pe_part, dve_part, act_part


def program(nc, io, stop_after=99, debug=None):
    root_ctx = ExitStack()
    with root_ctx:
        k = Core()
        keep_sem = lambda name: root_ctx.enter_context(nc.semaphore(name))
        block_sems = []

        def stage_sem(name):
            block_sems.append(nc.alloc_semaphore(name=name))
            return block_sems[-1]

        k.sem = stage_sem

        def sb(name, shape, dt=F, ctx=root_ctx):
            return ctx.enter_context(nc.sbuf_tensor(name, shape, dt))

        k.bank = [root_ctx.enter_context(nc.psum_tensor(f"bank{i}", [P, 512], F)) for i in range(8)]
        x = sb("x", [P, KT, S])
        k.raw = sb("w_raw", [P, 2, CW])
        k.whi = sb("w_hi_part", [P, 2, CW], R)
        k.wlo = sb("w_lo_part", [P, 2, CW], R)
        kept = sb("kept", [P, NKEPT])
        param = sb("param", [P, NPARAM])
        spread = sb("spread", [16, 8 * P])
        k.ones = sb("ones", [P, P])
        eps_col = sb("eps_col", [P, 1])
        mods = sb("mods", [P, 48])

        def c(name):
            a, b = CONST[name]
            return const[:, a:b]

        def pr(name):
            a, b = PARAM[name]
            return param[:, a:b]

        k.ident = kept[:, KEPT["ident"][0]:KEPT["ident"][1]]
        ind = kept[:, KEPT["ind"][0]:KEPT["ind"][1]].rearrange("p (t g) -> p t g", g=16)
        spread_v = spread[:, :].rearrange("g (t p) -> g t p", p=P)

        k.w_loaded = [keep_sem("w_loaded0"), keep_sem("w_loaded1")]
        k.w_hi, k.w_lo, k.w_used = keep_sem("w_hi"), keep_sem("w_lo"), keep_sem("w_used")
        x_in, const_in, param_in, set_up = keep_sem("x_in"), keep_sem("const_in"), keep_sem("param_in"), keep_sem("set_up")
        out_done = keep_sem("out_done")
        dve_own, act_own, pool_own = keep_sem("dve_own"), keep_sem("act_own"), keep_sem("pool_own")
        own = Own(dve_own)

        def dve_chain(eng):
            return Chain(eng, dve_own, own.dve)

        def act_chain(eng):
            return Chain(eng, act_own, own.act)

        def pool_chain(eng):
            return Chain(eng, pool_own, own.pool)

        def gone(ctx):
            ctx.close()

        G1 = 0
        proj_ctx = ExitStack()
        const = sb("const", [P, NCONST], ctx=proj_ctx)
        neg_ones = sb("neg_ones", [P, P], ctx=proj_ctx)
        proj = sb("proj", [P, 18, S], ctx=proj_ctx)
        v_stick = sb("v_stick", [P, NT, 256], ctx=proj_ctx)
        v_dil = sb("v_dil", [P, NT, 256], ctx=proj_ctx)
        v_nsa = sb("v_nsa", [P, NT, 140], ctx=proj_ctx)
        act_ctx = ExitStack()
        xhi = sb("xhi", [P, KT, S], R, act_ctx)
        xlo = sb("xlo", [P, KT, S], R, act_ctx)
        sq_ctx = ExitStack()
        k.sq = sb("sq", [P, 4, S], ctx=sq_ctx)
        k.root = sb("root", [P, S], ctx=sq_ctx)
        r1 = rms_signals(k, "r1")
        evac1a, evac1v = k.sem("evac1a"), k.sem("evac1v")

        with nc.Block() as block:

            @block.sync
            def _(sp):
                sp.dma_start(x[:, :, :], io["x"]).then_inc(x_in, 16)
                sp.dma_start(param[:, :], io["param"]).then_inc(param_in, 16)
                for g in range(2):
                    load_chunk(sp, k, g, io["w_in_f"][g])
                sp.dma_start(const[:, :], io["const"]).then_inc(const_in, 16)
                sp.dma_start(kept[:, :], io["kept"]).then_inc(const_in, 16)
                sp.dma_start(spread[:, :], io["spread"]).then_inc(const_in, 16)
                for g in range(2, 9):
                    load_chunk(sp, k, g % 2, io["w_in_f"][g], after_lo=g - 1)
                load_chunk(sp, k, 1, io["w_in_t"][0], after_lo=8)
                load_chunk(sp, k, 0, io["w_in_t"][1], after_lo=9)
                load_chunk(sp, k, 1, io["w_in_g"], after_lo=10)
                for g in range(12, 16):
                    load_chunk(sp, k, g % 2, io["w_out"][g - 12], after_lo=g - 1)
                sp.wait_ge(const_in, 48)

            @block.gpsimd
            def _(pool):
                nc.gpsimd.memset(k.ones[:, :], 1.0).then_inc(set_up, 1)
                nc.gpsimd.memset(eps_col[:, :], EPS).then_inc(set_up, 1)
                nc.gpsimd.memset(neg_ones[:, :], -1.0).then_inc(set_up, 1)

            @block.scalar
            def _(act):
                act.wait_ge(x_in, 16)
                act.wait_ge(set_up, 3)
                rms_act(act, k, lambda j: x[:, j, :], KT, r1, lambda j: xhi[:, j, :], eps_col[:, 0:1])
                for n in range(2):
                    round_chunk(act, k, n, 16, None)
                for g in range(12):
                    n = g + 2
                    round_chunk(act, k, n % 2, 16 * (n // 2 + 1), g + 1, KT * 140 if n == 11 else CW)
                    if g < 9:
                        out, ins = proj[:, 2 * g, :], k.bank[2 * (g % 2) + 0][:, :]
                        sc = 0.125 if 2 * g in (T_QC, T_QC + 1) else 1.0
                        act.activation(out, ins, ACT.Copy, scale=sc).then_inc(evac1a, 1)
                    else:
                        out = (v_stick, v_dil, v_nsa)[g - 9]
                        w = 140 if g == 11 else 256
                        for i in range(2):
                            ins = k.bank[4 * (g % 2) + i][:, 0:w]
                            last = act.activation(out[:, i, :], ins, ACT.Copy)
                        last.then_inc(evac1a, 1)

            @block.vector
            def _(dve):
                chain = dve_chain(dve)
                dve.wait_ge(param_in, 16)
                g_mix = pr("g_mix")
                rms_dve(dve, k, lambda j: x[:, j, :], KT, r1, lambda j: g_mix[:, j:j + 1], None,
                        lambda j: xlo[:, j, :], lambda j: xhi[:, j, :], chain)
                own.dve = chain.n
                for n in range(2):
                    rest_chunk(dve, k, n, n + 1)
                for g in range(12):
                    n = g + 2
                    rest_chunk(dve, k, n % 2, n + 1, KT * 140 if n == 11 else CW)
                    dve.wait_ge(k.w_used, g + 1)
                    if g < 9:
                        sc = 0.125 if 2 * g + 1 in (T_QC, T_QC + 1) else 1.0
                        dve.tensor_scalar(proj[:, 2 * g + 1, :], k.bank[2 * (g % 2) + 1][:, :], sc, None,
                                          ALU.mult).then_inc(evac1v, 1)
                    else:
                        out = (v_stick, v_dil, v_nsa)[g - 9]
                        w = 140 if g == 11 else 256
                        for i in range(2, 4):
                            last = dve.tensor_copy(out[:, i, :], k.bank[4 * (g % 2) + i][:, 0:w])
                        last.then_inc(evac1v, 1)

            @block.tensor
            def _(pe):
                pe.wait_ge(set_up, 3)
                rms_pe(pe, k, KT, r1)
                pe.wait_ge(r1.split, KT)
                for g in range(12):
                    pe.wait_ge(k.w_lo, g + 1)
                    if g >= 2:
                        pe.wait_ge(evac1a, g - 1)
                        pe.wait_ge(evac1v, g - 1)
                    if g < 9:
                        mm = pe_tiles(pe, k, g % 2, [k.bank[2 * (g % 2) + t][:, :] for t in range(2)], xhi, xlo)
                    else:
                        w = 140 if g == 11 else 256
                        mm = pe_tokens(pe, k, g % 2, w, [k.bank[4 * (g % 2) + i][:, 0:w] for i in range(NT)],
                                       xhi, xlo)
                    mm.then_inc(k.w_used, 1)
        gone(sq_ctx)
        gone(act_ctx)
        if debug and stop_after == 1:
            debug(nc, dict(proj=proj, v_stick=v_stick, v_dil=v_dil, v_nsa=v_nsa))
            gone(proj_ctx)
            return

        heads_ctx = ExitStack()
        o_all = sb("o_all", [P, 8, S], ctx=heads_ctx)
        kx = sb("kx", [P, S], ctx=heads_ctx)
        k_cmp = sb("k_cmp", [P, NCMP], ctx=heads_ctx)
        v_cmp = sb("v_cmp", [NCMP, HD], ctx=heads_ctx)
        gates = sb("gates", [P, NT, 12], ctx=heads_ctx)
        root16 = sb("root16", [16, S], ctx=heads_ctx)
        tmp_ctx = ExitStack()
        w1 = sb("w1", [P, 2, 16 * 256], ctx=tmp_ctx)
        windows = sb("windows", [P, 2, 16, NCMP], ctx=tmp_ctx)
        hid = sb("hid", [P, 4, NCMP], ctx=tmp_ctx)
        sq_cmp = sb("sq_cmp", [P, 2, NCMP], ctx=tmp_ctx)
        h_sq, h_sum, h_root, h_inv, h_wide, h_scaled, h_done = (k.sem(f"heads_{w}") for w in
                                                      ("squared", "summed", "rooted", "inverted", "spread", "scaled", "done"))
        w1_in, win_made, c_hid, c_gelu, c_out, c_sq, c_sum, c_root, g_sum, tmp_out = (
            k.sem(w) for w in ("w1_in", "windows_made", "cmp_hidden", "cmp_gelu", "cmp_out", "cmp_squared",
                               "cmp_summed", "cmp_rooted", "gate_sum", "tmp_out"))
        NH = len(NORMED)
        g_heads = pr("g_heads")
        pe_cols = pr("pe").rearrange("p (h j) -> p h j", h=2)
        w2k = pr("w2k").rearrange("p (c n) -> p c n", c=2)
        w2v = pr("w2v").rearrange("p (c n) -> p c n", c=2)

        with nc.Block() as block:

            @block.sync
            def _(sp):
                sp.dma_start(w1[:, 0, :], io["w1k"]).then_inc(w1_in, 16)
                sp.dma_start(w1[:, 1, :], io["w1v"]).then_inc(w1_in, 16)
                sp.wait_ge(w1_in, 32)

            @block.scalar
            def _(act):
                for n, t in enumerate(NORMED):
                    act.activation(o_all[:, n, :], proj[:, t, :], ACT.Square).then_inc(h_sq, 1)
                act.wait_ge(h_sum, 1)
                act.activation(root16[:, :], k.bank[0][0:16, :], ACT.Sqrt, bias=eps_col[0:16, 0:1],
                               scale=1.0 / HD).then_inc(h_root, 1)
                act.wait_ge(g_sum, 1)
                act.activation(gates[:, :, :], gates[:, :, :], ACT.Sigmoid).then_inc(g_sum, 1)
                act.wait_ge(c_hid, 1)
                act.activation(hid[:, :, :], k.bank[4][:, 0:4 * NCMP].rearrange("p (a n) -> p a n", n=NCMP),
                               ACT.Gelu_apprx_tanh).then_inc(c_gelu, 1)
                act.wait_ge(c_out, 1)
                act.activation(sq_cmp[:, 0, :], k.bank[5][:, 0:NCMP], ACT.Square).then_inc(c_sq, 1)
                act.wait_ge(c_sum, 1)
                act.activation(sq_cmp[:, 1, :], k.bank[6][:, 0:NCMP], ACT.Sqrt, bias=eps_col[:, 0:1],
                               scale=1.0 / P).then_inc(c_root, 1)
                act.activation(v_cmp[:, :], k.bank[7][0:NCMP, 64:128], ACT.Copy).then_inc(c_root, 1)

            @block.vector
            def _(dve):
                chain = dve_chain(dve)
                for kv in range(2):
                    rows = slice(HD * kv, HD * kv + HD)
                    toks = proj[rows, T_CV, :].rearrange("p (n l) -> p l n", l=16)
                    for par in range(2):
                        for half in range(2):
                            ins = dve.tensor_tensor(
                                windows[HD * par:HD * par + HD, kv, 8 * half:8 * half + 8, :],
                                toks[:, par:16:2, half:half + NCMP],
                                pe_cols[rows, par, 8 * half:8 * half + 8].unsqueeze(2).broadcast_to([HD, 8, NCMP]),
                                ALU.add)
                            ins.then_inc(win_made, 1)
                dve.tensor_tensor(gates[:, :, :], v_nsa[:, :, P:P + 12],
                                  pr("b_gate").rearrange("p (i g) -> p i g", i=NT), ALU.add).then_inc(g_sum, 1)
                for a, b in ((0, 2), (3, 5)):
                    last = chain.mark(dve.tensor_scalar(g_heads[:, a:b], g_heads[:, a:b], HD ** -0.5, None, ALU.mult))
                chain.need(last)
                dve.wait_ge(h_root, 1)
                dve.reciprocal(root16[:, :], root16[:, :]).then_inc(h_inv, 1)
                for n, t in enumerate(NORMED):
                    dve.wait_ge(h_wide, n + 1)
                    dve.scalar_tensor_tensor(
                        out=proj[:, t, :], in0=k.bank[1 + n % 3][:, :], scalar=g_heads[:, n:n + 1],
                        in1=proj[:, t, :], op0=ALU.mult, op1=ALU.mult).then_inc(h_scaled, 1)
                dve.wait_ge(h_scaled, 3)
                dve.tensor_copy(kx[0:HD, :], proj[HD:P, T_KSW, :]).then_inc(h_done, 1)
                dve.tensor_copy(kx[HD:P, :], proj[0:HD, T_KSW, :]).then_inc(h_done, 1)
                dve.wait_ge(c_root, 1)
                chain.link(dve.reciprocal(sq_cmp[:, 1, :], sq_cmp[:, 1, :]))
                dve.scalar_tensor_tensor(out=k_cmp[:, :], in0=k.bank[5][:, 0:NCMP], scalar=pr("g_kcmp"),
                                         in1=sq_cmp[:, 1, :], op0=ALU.mult, op1=ALU.mult).then_inc(h_done, 1)
                own.dve = chain.n

            @block.tensor
            def _(pe):
                for n in range(NH):
                    pe.wait_ge(h_sq, n + 1)
                    mm = pe.matmul(k.bank[0][0:16, :], ind[:, n, :], o_all[:, n, :], start=(n == 0), stop=(n == NH - 1))
                mm.then_inc(h_sum, 1)
                pe.wait_ge(w1_in, 32)
                pe.wait_ge(win_made, 8)
                for kv in range(2):
                    for ct in range(2):
                        a = (2 * kv + ct) * NCMP
                        for j in range(16):
                            mm = pe.matmul(k.bank[4][:, a:a + NCMP], w1[:, kv, 256 * j + P * ct:256 * j + P * ct + P],
                                           windows[:, kv, j, :], start=(j == 0), stop=(j == 15))
                mm.then_inc(c_hid, 1)
                pe.wait_ge(h_inv, 1)
                for n in range(NH):
                    if n >= 3:
                        pe.wait_ge(h_scaled, n - 2)
                    pe.matmul(k.bank[1 + n % 3][:, :], spread_v[:, n, :], root16[:, :], start=True,
                              stop=True).then_inc(h_wide, 1)
                pe.wait_ge(c_gelu, 1)
                for ct in range(2):
                    pe.matmul(k.bank[5][:, 0:NCMP], w2k[:, ct, :], hid[:, ct, :], start=(ct == 0), stop=(ct == 1))
                for ct in range(2):
                    mm = pe.matmul(k.bank[7][0:NCMP, 64:128], hid[:, 2 + ct, :], w2v[:, ct, :], start=(ct == 0),
                                   stop=(ct == 1))
                mm.then_inc(c_out, 1)
                pe.wait_ge(c_sq, 1)
                pe.matmul(k.bank[6][:, 0:NCMP], k.ones[:, :], sq_cmp[:, 0, :], start=True, stop=True).then_inc(c_sum, 1)
        gone(tmp_ctx)
        if debug and stop_after == 2:
            debug(nc, dict(proj=proj, kx=kx, k_cmp=k_cmp, v_cmp=v_cmp, gates=gates))
            gone(heads_ctx)
            gone(proj_ctx)
            return

        att_ctx = ExitStack()
        tables = sb("tables", [P, 8, S], ctx=att_ctx)
        ctab = sb("ctab", [P, 4, NT * NCMP], ctx=att_ctx)
        pc = sb("pc", [P, 4, NT, NCMP], ctx=att_ctx)
        pcT = sb("pcT", [NCMP, 4, S], ctx=att_ctx)
        cstat = sb("cstat", [P, 2, 16], ctx=att_ctx)
        conv_t = sb("conv_t", [P, 2, S], ctx=att_ctx)
        k.prob = sb("prob", [P, 4, S], ctx=att_ctx)
        k.probT = sb("probT", [P, 2, NT, S], ctx=att_ctx)
        k.nmax = sb("nmax", [P, 48], ctx=att_ctx)
        k.rsum = sb("rsum", [P, 48], ctx=att_ctx)
        tab_made, s_c, b_c, e_c, n_c, t_c, m_c = (k.sem(w) for w in (
            "tables_made", "cmp_scored", "cmp_biased", "cmp_exped", "cmp_normed", "cmp_turned", "cmp_moved"))
        conv_done = k.sem("conv_done")

        def head(tile, h):
            return proj[HD * (h % 2):HD * (h % 2) + HD, tile + h // 2, :]

        units, branches = [], []
        for hb in range(12):
            h, kind = (hb // 2, hb % 2) if hb < 8 else (hb - 8, 2)
            rows = slice(HD * (h % 2), HD * (h % 2) + HD)
            same = kind == h % 2
            keys = head(T_KD, h) if kind == 2 else (proj[rows, T_KSW, :] if same else kx[rows, :])
            qrow = head(T_QD, h) if kind == 2 else head(T_QA, h)
            for i in range(NT):
                w = P * (i + 1)
                gate = None if kind == 2 else gates[:, i, 3 * h + 1 + kind:3 * h + 2 + kind]
                units.append(Unit(branch=hb, i=i, q=qrow[:, P * i:P * i + P], key=keys[:, 0:w], width=w,
                                             blocks=list(range(i + 1)), gate=gate,
                                             table=tables[:, h + (4 if kind == 2 else 0), S - w:S]))

            def products(probT, h=h, kind=kind):
                for kt in range(NT):
                    v = v_dil[:, kt, HD * h:HD * h + HD] if kind == 2 else v_nsa[:, kt, HD * kind:HD * kind + HD]
                    yield (v, probT[:, kt, P * kt:S], P * kt, S, kind == 2 and kt == 0)

            branches.append(Branch(
                group=h if kind < 2 else 4 + h, first=kind != 1, stop=kind != 0, products=products,
                extra=(v_cmp[:, :], pcT[:, h, :]) if kind == 0 else None,
                out=o_all[rows, (0 if kind < 2 else 6) + h // 2, :]))
        pe_part, dve_part, act_part = attention(k, "att", units, branches, tab_made)

        with nc.Block() as block:

            @block.gpsimd
            def _(pool):
                chain = pool_chain(pool)
                taps = pr("conv").rearrange("p (t a) -> p t a", t=2)
                for t in range(2):
                    y, m, part = o_all[:, 2 + t, :], conv_t[:, 0, :], conv_t[:, 1, :]
                    chain.link(pool.tensor_tensor(m, proj[:, T_CC + t, :], proj[:, T_CU + t, :], ALU.mult))
                    chain.link(pool.tensor_scalar(y, m, taps[:, t, 2:3], None, ALU.mult))
                    for back in (1, 2):
                        chain.link(pool.tensor_scalar(part, m, taps[:, t, 2 - back:3 - back], None, ALU.mult))
                        chain.link(pool.tensor_tensor(y[:, back:S], y[:, back:S], part[:, 0:S - back], ALU.add))
                    chain.link(pool.tensor_tensor(y, y, proj[:, T_CB + t, :], ALU.mult))
                own.pool = chain.n

            @block.vector
            def _(dve):
                chain = dve_chain(dve)
                for h in range(4):
                    dve.scalar_tensor_tensor(out=ctab[:, h, :], in0=c("cdist"), scalar=-(2.0 ** -(2 * h + 1)),
                                             in1=c("cmask"), op0=ALU.mult, op1=ALU.add).then_inc(tab_made, 1)
                dve.wait_ge(s_c, 1)
                dve.wait_ge(tab_made, 4)
                for h in range(4):
                    a = NT * NCMP * (h // 2)
                    mark = chain.mark(dve.tensor_tensor(
                        pc[:, h, :, :].rearrange("p i n -> p (i n)"), k.bank[7 - h % 2][:, a:a + NT * NCMP],
                        ctab[:, h, :], ALU.add))
                pc16 = pc[:, :, :, :].rearrange("p h i n -> p (h i) n")
                chain.need(mark)
                chain.link(dve.tensor_reduce(cstat[:, 0, :], pc16, AX.X, ALU.max, negate=True))
                dve.tensor_tensor(pc16, pc16, cstat[:, 0, :].unsqueeze(2).broadcast_to([P, 16, NCMP]),
                                  ALU.add).then_inc(b_c, 1)
                for h in range(4):
                    for d in range(2):
                        dve.scalar_tensor_tensor(out=tables[:, 4 * d + h, :], in0=c("dist"),
                                                 scalar=-(2.0 ** -(2 * h + 1 + d)),
                                                 in1=c("dilated" if d else "causal"), op0=ALU.mult,
                                                 op1=ALU.add).then_inc(tab_made, 1)
                dve.wait_ge(e_c, 1)
                chain.link(dve.tensor_reduce(cstat[:, 1, :], pc16, AX.X, ALU.add))
                chain.link(dve.reciprocal(cstat[:, 1, :], cstat[:, 1, :]))
                hi4 = cstat[:, 1, :].rearrange("p (h i) -> p h i", h=4)
                cgate = gates[:, :, :].rearrange("p i (h b) -> p h i b", b=3)[:, :, :, 0]
                chain.link(dve.tensor_tensor(hi4, hi4, cgate, ALU.mult))
                chain.link(dve.tensor_tensor(pc16, pc16, cstat[:, 1, :].unsqueeze(2).broadcast_to([P, 16, NCMP]),
                                             ALU.mult))
                for h in range(4):
                    mark = dve.tensor_tensor(pc[:, h, :, :].rearrange("p i n -> p (i n)"),
                                             pc[:, h, :, :].rearrange("p i n -> p (i n)"), c("cvis"), ALU.mult)
                    mark.then_inc(n_c, 1)
                dve.wait_ge(tab_made, 12)
                dve_part(dve, chain)
                own.dve = chain.n

            @block.scalar
            def _(act):
                act.wait_ge(b_c, 1)
                act.activation(pc[:, :, :, :], pc[:, :, :, :], ACT.Exp).then_inc(e_c, 1)
                for h in range(4):
                    act.wait_ge(t_c, h + 1)
                    act.activation(pcT[:, h, :], k.bank[2 + h][0:NCMP, :], ACT.Copy).then_inc(m_c, 1)
                act_part(act)

            @block.tensor
            def _(pe):
                for h in range(4):
                    rows = slice(HD * (h % 2), HD * (h % 2) + HD)
                    for i in range(NT):
                        a = (h // 2 * NT + i) * NCMP
                        mm = pe.matmul(k.bank[7 - h % 2][:, a:a + NCMP], head(T_QA, h)[:, P * i:P * i + P], k_cmp[rows, :],
                                       start=True, stop=True)
                mm.then_inc(s_c, 1)
                for h in range(4):
                    pe.wait_ge(n_c, h + 1)
                    for i in range(NT):
                        mm = pe.transpose(k.bank[2 + h][0:NCMP, P * i:P * i + P], pc[:, h, i, :], k.ident)
                    mm.then_inc(t_c, 1)
                pe.wait_ge(m_c, 4)
                pe_part(pe)
        gone(att_ctx)
        if debug and stop_after == 3:
            debug(nc, dict(o_all=o_all))
            gone(heads_ctx)
            gone(proj_ctx)
            return

        stick_ctx = ExitStack()
        keep = sb("keep", [P, 2, NT, S], ctx=stick_ctx)
        soft = sb("soft", [P, 2, NT, S], ctx=stick_ctx)
        attn = sb("attn", [P, 2, NT, S], ctx=stick_ctx)
        st_z, st_ln, st_keep, st_rest, st_exp, st_out, st_stored = (
            k.sem(f"stick_{w}") for w in ("scored", "logged", "kept", "summed", "exped", "multiplied", "stored"))

        def stick_bank(h, kt):
            return k.bank[4 * (h % 2) + kt]

        with nc.Block() as block:

            @block.tensor
            def _(pe):
                def scores(h):
                    if h >= 2:
                        pe.wait_ge(st_stored, h - 1)
                    rows = slice(HD * (h % 2), HD * (h % 2) + HD)
                    for kt in range(NT):
                        pe.matmul(stick_bank(h, kt)[:, P * kt:S], head(T_KC, h)[:, P * kt:P * kt + P],
                                  head(T_QC, h)[:, P * kt:S], start=True, stop=True).then_inc(st_z, 1)

                def rest(h):
                    pe.wait_ge(st_keep, NT * (h + 1))
                    for kt in range(NT):
                        bank = stick_bank(h, kt)
                        pe.matmul(bank[:, P * kt:S], c("negtri"), keep[:, h % 2, kt, P * kt:S], start=False,
                                  stop=True, skip_group_check=True)
                        for later in range(kt + 1, NT):
                            pe.matmul(bank[:, P * later:S], neg_ones[:, :], keep[:, h % 2, later, P * later:S],
                                      start=False, stop=True, skip_group_check=True)
                        pe.matmul(bank[:, P * kt:P * kt + P], k.ident, c("future"), start=False, stop=True,
                                  skip_group_check=True).then_inc(st_rest, 1)

                def values(h):
                    pe.wait_ge(st_exp, NT * (h + 1))
                    for kt in range(NT):
                        mm = pe.matmul(stick_bank(h, 3)[0:HD, P * kt:S], v_stick[:, kt, HD * h:HD * h + HD],
                                       attn[:, h % 2, kt, P * kt:S], start=(kt == 0), stop=True,
                                       skip_group_check=kt > 0)
                    mm.then_inc(st_out, 1)

                scores(0)
                for h in range(4):
                    if h + 1 < 4:
                        scores(h + 1)
                    rest(h)
                    values(h)

            @block.scalar
            def _(act):
                def logs(h):
                    chain = act_chain(act)
                    t = [soft[:, h % 2, kt, P * kt:S] for kt in range(NT)]
                    marks = []
                    for kt in range(NT):
                        act.wait_ge(st_z, NT * h + kt + 1)
                        marks.append(chain.mark(act.activation(t[kt], stick_bank(h, kt)[:, P * kt:S], ACT.Abs)))
                    for kt in range(NT):
                        chain.need(marks[kt])
                        marks[kt] = chain.mark(act.activation(t[kt], t[kt], ACT.Exp, scale=-1.0))
                    for kt in range(NT):
                        chain.need(marks[kt])
                        act.activation(t[kt], t[kt], ACT.Ln, bias=1.0).then_inc(st_ln, 1)
                    own.act = chain.n

                def exps(h):
                    for kt in range(NT):
                        act.wait_ge(st_rest, NT * h + kt + 1)
                        act.activation(attn[:, h % 2, kt, P * kt:S], stick_bank(h, kt)[:, P * kt:S],
                                       ACT.Exp).then_inc(st_exp, 1)

                logs(0)
                for h in range(4):
                    if h + 1 < 4:
                        if h >= 1:
                            act.wait_ge(st_out, h)
                            act.activation(o_all[HD * ((h - 1) % 2):HD * ((h - 1) % 2) + HD, 4 + (h - 1) // 2, :],
                                           stick_bank(h - 1, 3)[0:HD, :], ACT.Copy).then_inc(st_stored, 1)
                        logs(h + 1)
                    exps(h)
                for h in (2, 3):
                    act.wait_ge(st_out, h + 1)
                    act.activation(o_all[HD * (h % 2):HD * (h % 2) + HD, 4 + h // 2, :],
                                   stick_bank(h, 3)[0:HD, :], ACT.Copy).then_inc(st_stored, 1)

            @block.vector
            def _(dve):
                chain = dve_chain(dve)
                for h in range(4):
                    for kt in range(NT):
                        dve.wait_ge(st_ln, NT * h + kt + 1)
                        if h >= 2:
                            dve.wait_ge(st_rest, NT * (h - 1))
                        t = keep[:, h % 2, kt, P * kt:S]
                        chain.link(dve.scalar_tensor_tensor(out=t, in0=stick_bank(h, kt)[:, P * kt:S], scalar=0.0,
                                                            in1=soft[:, h % 2, kt, P * kt:S], op0=ALU.max,
                                                            op1=ALU.add))
                        own_block = keep[:, h % 2, kt, P * kt:P * kt + P]
                        dve.tensor_tensor(own_block, own_block, c("past"), ALU.mult).then_inc(st_keep, 1)
                own.dve = chain.n
        gone(stick_ctx)
        if debug and stop_after == 4:
            debug(nc, dict(o_all=o_all))
            gone(heads_ctx)
            gone(proj_ctx)
            return

        out_ctx = ExitStack()
        ghi = sb("ghi", [P, KT, S], R, out_ctx)
        glo = sb("glo", [P, KT, S], R, out_ctx)
        gsq = sb("gsq", [P, KT, S], ctx=out_ctx)
        gn_sq, gn_sum, gn_root, gn_inv, gn_wide, gn_scaled, gn_hi, gn_lo, res1 = (
            k.sem(f"group_{w}") for w in ("squared", "summed", "rooted", "inverted", "spread", "scaled", "rounded",
                                          "split", "added"))
        G2 = 12

        with nc.Block() as block:

            @block.sync
            def _(sp):
                for g in range(G2 + 4, G2 + 8):
                    load_chunk(sp, k, g % 2, io["w_gu"][g - G2 - 4], after_lo=g - 1)

            @block.scalar
            def _(act):
                for j in range(8):
                    act.activation(gsq[:, j, :], o_all[:, j, :], ACT.Square).then_inc(gn_sq, 1)
                act.wait_ge(gn_sum, 1)
                act.activation(root16[:, :], k.bank[0][0:16, :], ACT.Sqrt, bias=eps_col[0:16, 0:1],
                               scale=1.0 / HD).then_inc(gn_root, 1)
                for j in range(8):
                    act.wait_ge(gn_scaled, j + 1)
                    act.activation(ghi[:, j, :], o_all[:, j, :], ACT.Copy).then_inc(gn_hi, 1)
                for n in range(G2 + 2, G2 + 6):
                    round_chunk(act, k, n % 2, 16 * (n // 2 + 1), n - 1)

            @block.vector
            def _(dve):
                dve.wait_ge(gn_root, 1)
                dve.reciprocal(root16[:, :], root16[:, :]).then_inc(gn_inv, 1)
                for j in range(8):
                    dve.wait_ge(gn_wide, j + 1)
                    dve.scalar_tensor_tensor(out=o_all[:, j, :], in0=k.bank[1 + j % 3][:, :],
                                             scalar=pr("g_out")[:, j:j + 1], in1=o_all[:, j, :], op0=ALU.mult,
                                             op1=ALU.mult).then_inc(gn_scaled, 1)
                for j in range(8):
                    dve.wait_ge(gn_hi, j + 1)
                    dve.tensor_tensor(glo[:, j, :], o_all[:, j, :], ghi[:, j, :].bitcast(F),
                                      ALU.subtract).then_inc(gn_lo, 1)
                for g in range(G2, G2 + 4):
                    rest_chunk(dve, k, g % 2, g + 3)
                    dve.wait_ge(k.w_used, g + 1)
                    for t in range(2):
                        j = 2 * (g - G2) + t
                        last = dve.tensor_tensor(x[:, j, :], x[:, j, :], k.bank[4 + 2 * (g % 2) + t][:, :], ALU.add)
                    last.then_inc(res1, 1)

            @block.tensor
            def _(pe):
                for j in range(8):
                    pe.wait_ge(gn_sq, j + 1)
                    mm = pe.matmul(k.bank[0][0:16, :], ind[:, j, :], gsq[:, j, :], start=(j == 0), stop=(j == 7))
                mm.then_inc(gn_sum, 1)
                pe.wait_ge(gn_inv, 1)
                for j in range(8):
                    if j >= 3:
                        pe.wait_ge(gn_scaled, j - 2)
                    pe.matmul(k.bank[1 + j % 3][:, :], spread_v[:, j, :], root16[:, :], start=True,
                              stop=True).then_inc(gn_wide, 1)
                pe.wait_ge(gn_lo, 8)
                for g in range(G2, G2 + 4):
                    pe.wait_ge(k.w_lo, g + 1)
                    if g >= G2 + 2:
                        pe.wait_ge(res1, g - G2 - 1)
                    pe_tiles(pe, k, g % 2, [k.bank[4 + 2 * (g % 2) + t][:, :] for t in range(2)], ghi,
                             glo).then_inc(k.w_used, 1)
        gone(out_ctx)
        gone(heads_ctx)
        gone(proj_ctx)
        if debug and stop_after == 5:
            debug(nc, dict(x=x))
            return

        GU, DN = G2 + 4, G2 + 4 + FT
        h_ctx = ExitStack()
        hhi = sb("hhi", [P, FT, S], R, h_ctx)
        hlo = sb("hlo", [P, FT, S], R, h_ctx)
        ffn_ctx = ExitStack()
        xhi = sb("xhi_ffn", [P, KT, S], R, ffn_ctx)
        xlo = sb("xlo_ffn", [P, KT, S], R, ffn_ctx)
        k.sq = sb("sq_ffn", [P, 4, S], ctx=ffn_ctx)
        k.root = sb("root_ffn", [P, S], ctx=ffn_ctx)
        hidden_stage(nc, k, "ffn", x, xhi, xlo, hhi, hlo,
                     (rms_signals(k, "r2"), lambda j: pr("g_ffn")[:, j:j + 1], None, eps_col[:, 0:1]),
                     GU, io["w_gu"], io["w_down"], None, own)
        gone(ffn_ctx)

        mod_ctx = ExitStack()
        modulation = Modulation(k, io, sb, mod_ctx, pr, mods)
        down_stage(nc, k, "down", x, hhi, hlo, DN, io["w_down"], io["w_in2"], None, modulation, None)
        gone(mod_ctx)
        gone(h_ctx)
        nc.clear_and_free_semaphores(block_sems)
        nc.all_engine_barrier()
        if debug and stop_after == 6:
            debug(nc, dict(x=x, mods=mods))
            return

        IN2 = DN + 2 * KT
        GLU, OUT2, UP2, DN2 = IN2 + 5, IN2 + 6, IN2 + 10, IN2 + 10 + FT
        mix_ctx = ExitStack()
        k.sq = sb("sq_mix", [P, 4, S], ctx=mix_ctx)
        k.root = sb("root_mix", [P, S], ctx=mix_ctx)
        proj2 = sb("proj2", [P, 9, S], ctx=mix_ctx)
        v2 = sb("v2", [P, NT, P], ctx=mix_ctx)
        y = sb("y", [P, 8, S], ctx=mix_ctx)
        bias_ctx = ExitStack()
        hot = sb("hot", [33, 384], ctx=bias_ctx)
        rel = sb("rel", [33, 8], ctx=bias_ctx)
        rel_rows = sb("rel_rows", [8, 384], ctx=bias_ctx)
        bias2 = sb("bias2", [P, 8, 256], ctx=bias_ctx)
        hot_in, rel_made, rel_sb, rel_out, rel_in = (k.sem(w) for w in ("hot_in", "rel_made", "rel_copied",
                                                                        "rel_out", "rel_in"))
        in_ctx = ExitStack()
        xhi = sb("xhi_in2", [P, KT, S], R, in_ctx)
        xlo = sb("xlo_in2", [P, KT, S], R, in_ctx)
        r3 = rms_signals(k, "r3")
        gains, evac2a, evac2v = k.sem("gains"), k.sem("in2_stored_a"), k.sem("in2_stored_v")
        shift1, scale1, gate1, shift2, scale2, gate2 = (mods[:, 8 * n:8 * n + 8] for n in range(6))

        with nc.Block() as block:

            @block.gpsimd
            def _(pool):
                pool.dma_start(hot[:, :], io["hot"]).then_inc(hot_in, 16)
                pool.dma_start(rel[:, :], io["rel_bias"]).then_inc(hot_in, 16)
                pool.wait_ge(rel_sb, 1)
                pool.dma_start(io["rel_scratch"], rel_rows[:, :].unsqueeze(1).broadcast_to([8, P, 384]))\
                    .then_inc(rel_out, 16)
                pool.wait_ge(rel_out, 16)
                pool.dma_start(bias2[:, :, :], bass.AP(io["rel_scratch"].tensor, io["rel_scratch"].offset + P - 1,
                                                       [[383, P], [P * 384, 8], [1, 256]])).then_inc(rel_in, 16)
                pool.wait_ge(rel_in, 16)

            @block.sync
            def _(sp):
                for g in range(IN2 + 4, IN2 + 8):
                    src = io["w_in2"][g - IN2] if g < GLU else (io["w_glu"] if g == GLU else io["w_out2"][g - OUT2])
                    load_chunk(sp, k, g % 2, src, after_lo=g - 1)

            @block.scalar
            def _(act):
                act.wait_ge(rel_made, 1)
                act.activation(rel_rows[:, :], k.bank[7][0:8, 0:384], ACT.Copy).then_inc(rel_sb, 1)
                rms_act(act, k, lambda j: x[:, j, :], KT, r3, lambda j: xhi[:, j, :], eps_col[:, 0:1])
                for g in range(IN2, IN2 + 5):
                    n = g + 2
                    round_chunk(act, k, n % 2, 16 * (n // 2 + 1), n - 1)
                    act.activation(proj2[:, 2 * (g - IN2), :], k.bank[2 * (g % 2)][:, :], ACT.Copy).then_inc(evac2a, 1)

            @block.vector
            def _(dve):
                chain = dve_chain(dve)
                for scale, norm in ((scale1, "norm1"), (scale2, "norm2")):
                    last = chain.mark(dve.scalar_tensor_tensor(out=scale, in0=scale, scalar=1.0, in1=pr(norm),
                                                               op0=ALU.add, op1=ALU.mult))
                chain.need(last)
                rms_dve(dve, k, lambda j: x[:, j, :], KT, r3, lambda j: scale1[:, j:j + 1],
                        lambda j: shift1[:, j:j + 1], lambda j: xlo[:, j, :], lambda j: xhi[:, j, :], chain)
                for g in range(IN2, IN2 + 5):
                    rest_chunk(dve, k, g % 2, g + 3)
                    dve.wait_ge(k.w_used, g + 1)
                    if g < IN2 + 4:
                        last = dve.tensor_copy(proj2[:, 2 * (g - IN2) + 1, :], k.bank[2 * (g % 2) + 1][:, :])
                    else:
                        for i in range(NT):
                            last = dve.tensor_copy(v2[:, i, :], k.bank[4 + i][:, 0:P])
                    last.then_inc(evac2v, 1)
                own.dve = chain.n

            @block.tensor
            def _(pe):
                pe.wait_ge(hot_in, 32)
                pe.matmul(k.bank[7][0:8, 0:384], rel[:, :], hot[:, :], start=True, stop=True).then_inc(rel_made, 1)
                rms_pe(pe, k, KT, r3)
                pe.wait_ge(r3.split, KT)
                for g in range(IN2, IN2 + 4):
                    pe.wait_ge(k.w_lo, g + 1)
                    if g >= IN2 + 2:
                        pe.wait_ge(evac2a, g - IN2 - 1)
                        pe.wait_ge(evac2v, g - IN2 - 1)
                    pe_tiles(pe, k, g % 2, [k.bank[2 * (g % 2) + t][:, :] for t in range(2)], xhi,
                             xlo).then_inc(k.w_used, 1)
                g = IN2 + 4
                pe.wait_ge(k.w_lo, g + 1)
                pe.wait_ge(evac2a, 3)
                hi = k.whi[:, g % 2, :].rearrange("p (k n) -> p k n", n=256)
                lo = k.wlo[:, g % 2, :].rearrange("p (k n) -> p k n", n=256)
                for j in range(KT):
                    split_mm(pe, k.bank[2 * (g % 2)][:, :], hi[:, j, 0:P], lo[:, j, 0:P], xhi[:, j, :], xlo[:, j, :],
                             j == 0, j == KT - 1)
                for i in range(NT):
                    tok = slice(P * i, P * i + P)
                    for j in range(KT):
                        mm = split_mm(pe, k.bank[4 + i][:, 0:P], xhi[:, j, tok], xlo[:, j, tok], hi[:, j, P:256],
                                      lo[:, j, P:256], j == 0, j == KT - 1)
                mm.then_inc(k.w_used, 1)
        gone(in_ctx)
        if debug and stop_after == 7:
            debug(nc, dict(proj2=proj2, v2=v2, mods=mods))
            gone(bias_ctx)
            gone(mix_ctx)
            return

        swa_ctx = ExitStack()
        kx2 = sb("kx2", [P, S], ctx=swa_ctx)
        root10 = sb("root10", [16, S], ctx=swa_ctx)
        hsq = sb("hsq", [P, 5, S], ctx=swa_ctx)
        nsinks = sb("nsinks", [P, 8], ctx=swa_ctx)
        k.prob = sb("prob2", [P, 4, S], ctx=swa_ctx)
        k.probT = sb("probT2", [P, 2, NT, S], ctx=swa_ctx)
        k.nmax = sb("nmax2", [P, 32], ctx=swa_ctx)
        k.rsum = sb("rsum2", [P, 32], ctx=swa_ctx)
        k.esink = sb("esink", [P, 32], ctx=swa_ctx)
        h2_sq, h2_sum, h2_root, h2_inv, h2_wide, h2_scaled, h2_done = (
            k.sem(w) for w in ("heads2_squared",
                               "heads2_summed", "heads2_rooted", "heads2_inverted", "heads2_spread",
                               "heads2_scaled", "heads2_done"))
        units, branches = [], []
        for h in range(8):
            rows = slice(HD * (h % 2), HD * (h % 2) + HD)
            kv = h // 4
            keys = proj2[rows, 8, :] if kv == h % 2 else kx2[rows, :]
            for i in range(NT):
                w = P if i == 0 else 256
                units.append(Unit(branch=h, i=i, q=proj2[rows, 4 + h // 2, P * i:P * i + P],
                                             key=keys[:, P * (i + 1) - w:P * (i + 1)], width=w,
                                             blocks=[0] if i == 0 else [i - 1, i], 
                                             sink=pr("sinks")[:, h:h + 1], nsink=nsinks[:, h:h + 1],
                                             table=bias2[:, h, 256 - w:256]))

            def products(probT, kv=kv):
                for kt in range(NT):
                    end = min(S, P * kt + 256)
                    yield v2[:, kt, HD * kv:HD * kv + HD], probT[:, kt, P * kt:end], P * kt, end, kt == 0

            branches.append(Branch(group=h, products=products,
                                            out=y[rows, 4 + h // 2, :]))
        pe_part, dve_part, act_part = attention(k, "swa", units, branches, None)

        with nc.Block() as block:

            @block.scalar
            def _(act):
                for n in range(5):
                    act.activation(hsq[:, n, :], proj2[:, 4 + n, :], ACT.Square).then_inc(h2_sq, 1)
                act.wait_ge(h2_sum, 1)
                act.activation(root10[:, :], k.bank[0][0:16, :], ACT.Sqrt, bias=eps_col[0:16, 0:1],
                               scale=1.0 / HD).then_inc(h2_root, 1)
                act_part(act)

            @block.vector
            def _(dve):
                chain = dve_chain(dve)
                dve.tensor_scalar(nsinks[:, :], pr("sinks"), -1.0, None, ALU.mult).then_inc(h2_done, 1)
                g_heads2 = pr("g_heads2")
                chain.link(dve.tensor_scalar(g_heads2[:, 0:4], g_heads2[:, 0:4], HD ** -0.5, None, ALU.mult))
                dve.wait_ge(h2_root, 1)
                dve.reciprocal(root10[:, :], root10[:, :]).then_inc(h2_inv, 1)
                for n in range(5):
                    dve.wait_ge(h2_wide, n + 1)
                    dve.scalar_tensor_tensor(out=proj2[:, 4 + n, :], in0=k.bank[1 + n % 3][:, :],
                                             scalar=g_heads2[:, n:n + 1], in1=proj2[:, 4 + n, :],
                                             op0=ALU.mult, op1=ALU.mult).then_inc(h2_scaled, 1)
                dve.wait_ge(h2_scaled, 5)
                dve.tensor_copy(kx2[0:HD, :], proj2[HD:P, 8, :]).then_inc(h2_done, 1)
                dve.tensor_copy(kx2[HD:P, :], proj2[0:HD, 8, :]).then_inc(h2_done, 1)
                dve.wait_ge(h2_done, 3)
                dve_part(dve, chain)
                own.dve = chain.n

            @block.tensor
            def _(pe):
                for n in range(5):
                    pe.wait_ge(h2_sq, n + 1)
                    mm = pe.matmul(k.bank[0][0:16, :], ind[:, n, :], hsq[:, n, :], start=(n == 0), stop=(n == 4))
                mm.then_inc(h2_sum, 1)
                pe.wait_ge(h2_inv, 1)
                for n in range(5):
                    if n >= 3:
                        pe.wait_ge(h2_scaled, n - 2)
                    pe.matmul(k.bank[1 + n % 3][:, :], spread_v[:, n, :], root10[:, :], start=True,
                              stop=True).then_inc(h2_wide, 1)
                pe.wait_ge(h2_done, 3)
                pe_part(pe)
        gone(swa_ctx)
        gone(bias_ctx)
        if debug and stop_after == 8:
            debug(nc, dict(y=y))
            gone(mix_ctx)
            return

        ssm_ctx = ExitStack()
        ssm_b = sb("ssm_b", [P, 2, 4, P], ctx=ssm_ctx)
        ssm_c = sb("ssm_c", [P, 2, 16, 32], ctx=ssm_ctx)
        c_out = sb("c_out", [P, 3, 16, 32], ctx=ssm_ctx)
        c_tmp = sb("c_tmp", [P, 2, 16, 32], ctx=ssm_ctx)
        time = sb("time", [P, S], ctx=ssm_ctx)
        cols = sb("ssm_cols", [P, 24, 16], ctx=ssm_ctx)
        ang = sb("angle", [P, 2, 2, S], ctx=ssm_ctx)
        cs = sb("cos_sin", [P, 2, 2, S], ctx=ssm_ctx)
        rot = sb("rotated", [P, 4, S], ctx=ssm_ctx)
        w_st = sb("w_state", [P, 2, 2, S], ctx=ssm_ctx)
        back = sb("rotated_back", [P, 2, 4, S], ctx=ssm_ctx)
        z_sum = k.sq
        zhi = sb("zhi", [P, 4, S], R, ssm_ctx)
        zlo = sb("zlo", [P, 4, S], R, ssm_ctx)
        (sm_in, sm_col, sm_exp, sm_c, sm_ang, sm_sin, sm_cos, sm_bu, sm_rot, sm_w, sm_back, sm_y, sm_ysum, sm_z,
         sm_zhi, sm_zlo, sm_g, sm_sig, sm_done) = (k.sem(f"ssm_{w}") for w in (
             "in", "columns", "exp", "c_made", "angle", "sin", "cos", "bu", "rotated", "scanned", "back", "y",
             "y_sum", "z", "z_rounded", "z_split", "glu", "sigmoid", "done"))

        def col(n):
            return cols[:, n, :]

        LR, DT, XM, MAG, TH, KK, RED, SIN, HALFSIN, COS, ARE, AIM, DEN, FRE, FIM, TURN, TH_HI, TH_LO, T1, T2 = range(20)

        with nc.Block() as block:

            @block.sync
            def _(sp):
                sp.dma_start(ssm_b[:, :, :, :], io["ssm_b"].rearrange("p (a t n) -> p a t n", a=2, t=4)).then_inc(sm_in, 16)
                sp.dma_start(ssm_c[:, :, :, :], io["ssm_c"].rearrange("p (a t n) -> p a t n", a=2, t=16)).then_inc(sm_in, 16)
                sp.dma_start(time[:, :], io["time"]).then_inc(sm_in, 16)
                for g in range(OUT2 + 2, OUT2 + 4):
                    load_chunk(sp, k, g % 2, io["w_out2"][g - OUT2], after_lo=g - 1)
                sp.wait_ge(sm_in, 48)

            @block.scalar
            def _(act):
                act.activation(col(DT), pr("log_dt"), ACT.Exp).then_inc(sm_exp, 1)
                act.wait_ge(sm_col, 1)
                act.activation(col(MAG), col(XM), ACT.Exp).then_inc(sm_exp, 1)
                act.wait_ge(sm_col, 2)
                act.activation(col(SIN), col(RED), ACT.Sin).then_inc(sm_exp, 1)
                act.activation(col(HALFSIN), col(RED), ACT.Sin, scale=0.5).then_inc(sm_exp, 1)
                chain = act_chain(act)
                for i in range(16):
                    act.wait_ge(sm_ang, i + 1)
                    if i >= 2:
                        act.wait_ge(sm_back, 4 * (i - 1))
                    act.activation(cs[:, i % 2, 1, :], ang[:, i % 2, 0, :], ACT.Sin, scale=6.283185).then_inc(sm_sin, 1)
                    chain.link(act.activation(ang[:, i % 2, 1, :], ang[:, i % 2, 0, :], ACT.Sin, scale=3.1415925))
                    act.activation(ang[:, i % 2, 1, :], ang[:, i % 2, 1, :], ACT.Square).then_inc(sm_sin, 1)
                own.act = chain.n
                for t in range(4):
                    act.wait_ge(sm_ysum, t + 1)
                    chain = act_chain(act)
                    chain.link(act.activation(z_sum[:, t, :], z_sum[:, t, :], ACT.Gelu_apprx_tanh))
                    own.act = chain.n
                    act.activation(zhi[:, t, :], z_sum[:, t, :], ACT.Copy).then_inc(sm_zhi, 1)
                round_chunk(act, k, (OUT2 + 1) % 2, 16 * ((OUT2 + 1) // 2 + 1), OUT2)
                for t in range(4):
                    act.activation(y[:, t, :], k.bank[t][:, :], ACT.Sigmoid,
                                   bias=pr("b_glu")[:, t:t + 1]).then_inc(sm_sig, 1)

            @block.vector
            def _(dve):
                chain = dve_chain(dve)

                def ts(out, a, s1, s2, op0, op1=None):
                    chain.link(dve.tensor_scalar(out, a, s1, s2, op0, op1) if op1 is not None
                               else dve.tensor_scalar(out, a, s1, s2, op0))

                def tt(out, a, b, op):
                    chain.link(dve.tensor_tensor(out, a, b, op))

                def stt(out, a, s, b, op0, op1):
                    chain.link(dve.scalar_tensor_tensor(out=out, in0=a, scalar=s, in1=b, op0=op0, op1=op1))

                lam_im = pr("lam_im")
                ts(col(LR), pr("lam_re"), -1e-4, None, ALU.min)
                dve.wait_ge(sm_exp, 1)
                dve.tensor_tensor(col(XM), col(DT), col(LR), ALU.mult).then_inc(sm_col, 1)
                tt(col(TH), col(DT), lam_im, ALU.mult)
                ts(col(KK), col(TH), 1.0 / TWO_PI, ROUND, ALU.mult, ALU.add)
                ts(col(KK), col(KK), -ROUND, None, ALU.add)
                stt(col(RED), col(KK), -6.28125, col(TH), ALU.mult, ALU.add)
                stt(col(RED), col(KK), -(TWO_PI - 6.28125), col(RED), ALU.mult, ALU.add)
                dve.tensor_scalar(col(RED), col(RED), 3.1415925, -3.1415925, ALU.min, ALU.max).then_inc(sm_col, 1)
                dve.wait_ge(sm_col, 2)
                ts(col(TURN), col(RED), 1.0 / TWO_PI, None, ALU.mult)
                ts(col(TH_HI), col(TURN), 16384.0, ROUND, ALU.mult, ALU.add)
                ts(col(TH_HI), col(TH_HI), -ROUND, 1.0 / 16384.0, ALU.add, ALU.mult)
                tt(col(TH_LO), col(TURN), col(TH_HI), ALU.subtract)

                def angle(i):
                    a, b = ang[:, i % 2, 0, :], ang[:, i % 2, 1, :]
                    if i >= 2:
                        dve.wait_ge(sm_sin, 2 * (i - 1))
                        dve.wait_ge(sm_cos, i - 1)
                    ts(a, time[:, :], col(TURN)[:, i:i + 1], ROUND, ALU.mult, ALU.add)
                    ts(a, a, -ROUND, None, ALU.add)
                    stt(a, time[:, :], col(TH_HI)[:, i:i + 1], a, ALU.mult, ALU.subtract)
                    stt(a, time[:, :], col(TH_LO)[:, i:i + 1], a, ALU.mult, ALU.add)
                    dve.tensor_scalar(a, a, 0.5, -0.5, ALU.min, ALU.max).then_inc(sm_ang, 1)

                dve.wait_ge(sm_in, 48)
                angle(0)
                dve.wait_ge(sm_exp, 4)
                tt(col(COS), col(HALFSIN), col(HALFSIN), ALU.mult)
                ts(col(COS), col(COS), -2.0, 1.0, ALU.mult, ALU.add)
                tt(col(ARE), col(MAG), col(COS), ALU.mult)
                ts(col(ARE), col(ARE), -1.0, None, ALU.add)
                tt(col(AIM), col(MAG), col(SIN), ALU.mult)
                tt(col(DEN), col(LR), col(LR), ALU.mult)
                tt(col(T1), lam_im, lam_im, ALU.mult)
                tt(col(DEN), col(DEN), col(T1), ALU.add)
                chain.link(dve.reciprocal(col(DEN), col(DEN)))
                tt(col(FRE), col(ARE), col(LR), ALU.mult)
                tt(col(T1), col(AIM), lam_im, ALU.mult)
                tt(col(FRE), col(FRE), col(T1), ALU.add)
                tt(col(FRE), col(FRE), col(DEN), ALU.mult)
                tt(col(FIM), col(AIM), col(LR), ALU.mult)
                tt(col(T1), col(ARE), lam_im, ALU.mult)
                tt(col(FIM), col(FIM), col(T1), ALU.subtract)
                tt(col(FIM), col(FIM), col(DEN), ALU.mult)

                def wide(n):
                    return col(n).unsqueeze(2).broadcast_to([P, 16, 32])

                tt(c_tmp[:, 0, :, :], ssm_c[:, 0, :, :], wide(FRE), ALU.mult)
                tt(c_tmp[:, 1, :, :], ssm_c[:, 1, :, :], wide(FIM), ALU.mult)
                tt(c_out[:, 0, :, :], c_tmp[:, 0, :, :], c_tmp[:, 1, :, :], ALU.subtract)
                tt(c_out[:, 1, :, :], c_tmp[:, 1, :, :], c_tmp[:, 0, :, :], ALU.subtract)
                tt(c_tmp[:, 0, :, :], ssm_c[:, 0, :, :], wide(FIM), ALU.mult)
                tt(c_tmp[:, 1, :, :], ssm_c[:, 1, :, :], wide(FRE), ALU.mult)
                stt(c_out[:, 2, :, :], c_tmp[:, 0, :, :], -1.0, c_tmp[:, 1, :, :], ALU.mult, ALU.subtract)
                dve.sem_inc(sm_c, 1)

                for i in range(16):
                    if i + 1 < 16:
                        angle(i + 1)
                    cos, sin = cs[:, i % 2, 0, :], cs[:, i % 2, 1, :]
                    dve.wait_ge(sm_sin, 2 * (i + 1))
                    if i >= 2:
                        dve.wait_ge(sm_back, 4 * (i - 1))
                    dve.tensor_scalar(cos, ang[:, i % 2, 1, :], -2.0, 1.0, ALU.mult, ALU.add).then_inc(sm_cos, 1)
                    dve.wait_ge(sm_cos, i + 1)
                    dve.wait_ge(sm_bu, i + 1)
                    bre, bim = k.bank[2 * (i % 2)][:, :], k.bank[2 * (i % 2) + 1][:, :]
                    chain.mark(dve.tensor_tensor(rot[:, 0, :], bre, cos, ALU.mult))
                    chain.mark(dve.tensor_tensor(rot[:, 1, :], bim, sin, ALU.mult))
                    chain.mark(dve.tensor_tensor(rot[:, 2, :], bim, cos, ALU.mult))
                    m = chain.mark(dve.tensor_tensor(rot[:, 3, :], bre, sin, ALU.mult))
                    chain.need(m)
                    chain.mark(dve.tensor_tensor(rot[:, 0, :], rot[:, 0, :], rot[:, 1, :], ALU.add))
                    m = chain.mark(dve.tensor_tensor(rot[:, 2, :], rot[:, 2, :], rot[:, 3, :], ALU.subtract))
                    chain.need(m)
                    mag = col(MAG)[:, i:i + 1].broadcast_to([P, S])
                    for a in range(2):
                        dve.tensor_tensor_scan(w_st[:, i % 2, a, :], mag, rot[:, 2 * a, :], 0.0, ALU.mult,
                                               ALU.add).then_inc(sm_w, 1)
                    dve.wait_ge(sm_w, 2 * (i + 1))
                for t in range(4):
                    dve.wait_ge(sm_y, 4 * (t + 1))
                    dve.scalar_tensor_tensor(out=z_sum[:, t, :], in0=proj2[:, t, :], scalar=pr("d_skip")[:, t:t + 1],
                                             in1=k.bank[4 + t][:, :], op0=ALU.mult, op1=ALU.add).then_inc(sm_ysum, 1)
                for t in range(4):
                    dve.wait_ge(sm_zhi, t + 1)
                    dve.tensor_tensor(zlo[:, t, :], z_sum[:, t, :], zhi[:, t, :].bitcast(F),
                                      ALU.subtract).then_inc(sm_zlo, 1)
                rest_chunk(dve, k, (OUT2 + 1) % 2, OUT2 + 2)
                for t in range(4):
                    dve.wait_ge(sm_sig, t + 1)
                    dve.tensor_tensor(y[:, t, :], y[:, t, :], z_sum[:, t, :], ALU.mult).then_inc(sm_done, 1)
                own.dve = chain.n

            @block.gpsimd
            def _(pool):
                for i in range(16):
                    cos, sin = cs[:, i % 2, 0, :], cs[:, i % 2, 1, :]
                    pool.wait_ge(sm_w, 2 * (i + 1))
                    if i >= 2:
                        pool.wait_ge(sm_y, i - 1)
                    for n, (a, table) in enumerate(((0, cos), (1, sin), (0, sin), (1, cos))):
                        pool.tensor_tensor(back[:, i % 2, n, :], w_st[:, i % 2, a, :], table, ALU.mult)\
                            .then_inc(sm_back, 1)

            @block.tensor
            def _(pe):
                def inputs(i):
                    r = slice(32 * (i % 4), 32 * (i % 4) + 32)
                    if i >= 2:
                        pe.wait_ge(sm_w, 2 * (i - 1))
                    for a in range(2):
                        mm = pe.matmul(k.bank[2 * (i % 2) + a][:, :], ssm_b[r, a, i // 4, :], proj2[r, i // 4, :],
                                       start=True, stop=True)
                    mm.then_inc(sm_bu, 1)

                pe.wait_ge(sm_in, 48)
                inputs(0)
                pe.wait_ge(sm_c, 1)
                for i in range(16):
                    if i + 1 < 16:
                        inputs(i + 1)
                    r = slice(32 * (i % 4), 32 * (i % 4) + 32)
                    for n, m in enumerate((0, 1, 2, 2)):
                        pe.wait_ge(sm_back, 4 * i + n + 1)
                        mm = pe.matmul(k.bank[4 + i // 4][r, :], c_out[:, m, i, :], back[:, i % 2, n, :],
                                       start=(n == 0), stop=(n == 3))
                    mm.then_inc(sm_y, 1)
                pe.wait_ge(sm_zlo, 4)
                pe.wait_ge(k.w_lo, GLU + 1)
                hi = k.whi[:, GLU % 2, :].rearrange("p (k n) -> p k n", n=S)
                lo = k.wlo[:, GLU % 2, :].rearrange("p (k n) -> p k n", n=S)
                for t in range(4):
                    for j in range(4):
                        mm = split_mm(pe, k.bank[t][:, :], hi[:, j, P * t:P * t + P], lo[:, j, P * t:P * t + P],
                                      zhi[:, j, :], zlo[:, j, :], j == 0, j == 3)
                mm.then_inc(k.w_used, 1)
        gone(ssm_ctx)
        if debug and stop_after == 9:
            debug(nc, dict(y=y))
            gone(mix_ctx)
            return

        out_ctx = ExitStack()
        xhi = sb("xhi_out2", [P, KT, S], R, out_ctx)
        xlo = sb("xlo_out2", [P, KT, S], R, out_ctx)
        r4, r5 = rms_signals(k, "r4"), rms_signals(k, "r5")
        res2 = k.sem("out2_added")

        with nc.Block() as block:

            @block.sync
            def _(sp):
                for g in range(UP2, UP2 + 4):
                    load_chunk(sp, k, g % 2, io["w_up2"][g - UP2], after_lo=g - 1)

            @block.scalar
            def _(act):
                rms_act(act, k, lambda j: y[:, j, :], 4, r4, lambda j: xhi[:, j, :], eps_col[:, 0:1])
                act.wait_ge(r4.split, 4)
                rms_act(act, k, lambda j: y[:, 4 + j, :], 4, r5, lambda j: xhi[:, 4 + j, :], eps_col[:, 0:1])
                for n in range(OUT2 + 2, OUT2 + 6):
                    round_chunk(act, k, n % 2, 16 * (n // 2 + 1), n - 1)

            @block.vector
            def _(dve):
                chain = dve_chain(dve)
                for first, sig, gain in ((0, r4, pr("o_ssm")), (4, r5, pr("o_attn"))):
                    rms_dve(dve, k, lambda j, first=first: y[:, first + j, :], 4, sig,
                            lambda j, gain=gain: gain[:, j:j + 1], None,
                            lambda j, first=first: xlo[:, first + j, :], lambda j, first=first: xhi[:, first + j, :],
                            chain)
                for g in range(OUT2, OUT2 + 4):
                    rest_chunk(dve, k, g % 2, g + 3)
                    dve.wait_ge(k.w_used, g + 1)
                    for t in range(2):
                        j = 2 * (g - OUT2) + t
                        last = dve.scalar_tensor_tensor(out=x[:, j, :], in0=k.bank[4 + 2 * (g % 2) + t][:, :],
                                                        scalar=gate1[:, j:j + 1], in1=x[:, j, :], op0=ALU.mult,
                                                        op1=ALU.add)
                    last.then_inc(res2, 1)
                own.dve = chain.n

            @block.tensor
            def _(pe):
                rms_pe(pe, k, 4, r4)
                pe.wait_ge(r4.rooted, 1)
                rms_pe(pe, k, 4, r5)
                pe.wait_ge(r5.split, 4)
                for g in range(OUT2, OUT2 + 4):
                    pe.wait_ge(k.w_lo, g + 1)
                    if g >= OUT2 + 2:
                        pe.wait_ge(res2, g - OUT2 - 1)
                    pe_tiles(pe, k, g % 2, [k.bank[4 + 2 * (g % 2) + t][:, :] for t in range(2)], xhi,
                             xlo).then_inc(k.w_used, 1)
        gone(out_ctx)
        gone(mix_ctx)
        if debug and stop_after == 10:
            debug(nc, dict(x=x))
            return

        h_ctx = ExitStack()
        hhi = sb("hhi2", [P, FT, S], R, h_ctx)
        hlo = sb("hlo2", [P, FT, S], R, h_ctx)
        ffn_ctx = ExitStack()
        xhi = sb("xhi_ffn2", [P, KT, S], R, ffn_ctx)
        xlo = sb("xlo_ffn2", [P, KT, S], R, ffn_ctx)
        k.sq = sb("sq_ffn2", [P, 4, S], ctx=ffn_ctx)
        k.root = sb("root_ffn2", [P, S], ctx=ffn_ctx)
        hidden_stage(nc, k, "ffn2", x, xhi, xlo, hhi, hlo,
                     (rms_signals(k, "r6"), lambda j: scale2[:, j:j + 1], lambda j: shift2[:, j:j + 1], eps_col[:, 0:1]),
                     UP2, io["w_up2"], io["w_down2"], (pr("convw2"), pr("convb2")), own)
        gone(ffn_ctx)
        down_stage(nc, k, "down2", x, hhi, hlo, DN2, io["w_down2"], None, gate2, None, io["out"])
        gone(h_ctx)



def constants():
    p, q = np.arange(P)[:, None], np.arange(P)[None, :]
    dist = p + (S - P) - np.arange(S)[None, :]
    ind = np.zeros((P, 8, 16))
    spread = np.zeros((16, 8, P))
    for t in range(8):
        for half in range(2):
            ind[64 * half:64 * half + 64, t, 2 * t + half] = 1
            spread[2 * t + half, t, 64 * half:64 * half + 64] = 1
    times = ((dist >= 0) & (dist <= P)).astype(int) + (dist % 4 == 0) + (dist % 16 == 0)
    dilated = np.where((dist >= 0) & (times > 0), np.log(np.maximum(times, 1)), NEG)
    cdist = (P * np.arange(NT)[None, :, None] + np.arange(P)[:, None, None]
             - (16 * np.arange(NCMP) + 31)[None, None, :]).reshape(P, -1)
    parts = {"ident": np.eye(P), "negtri": -(p >= q).astype(float), "past": (p < q).astype(float),
             "future": np.where(p < q, 0.0, NEG), "dist": dist, "causal": np.where(dist >= 0, 0.0, NEG),
             "dilated": dilated, "ind": ind.reshape(P, -1),
             "cdist": cdist, "cmask": np.where(cdist >= 0, 0.0, NEG), "cvis": (cdist >= 0).astype(float)}
    const = np.concatenate([np.asarray(parts[name], np.float32) for name in CONST], axis=1)
    n = 255 - np.arange(384)
    inside = (n >= 0) & (n < P)
    b = np.maximum(n, 0)
    large = 16 + (np.log(np.maximum(b, 1) / 16) / np.log(P / 16) * 16).astype(np.int32)
    bucket = np.where(b < 16, b, np.minimum(large, 31))
    hot = np.zeros((33, 384), np.float32)
    for j in range(384):
        if inside[j]:
            hot[bucket[j], j] = 1
        else:
            hot[32, j] = NEG
    kept = np.concatenate([np.asarray(parts[name], np.float32) for name in KEPT], axis=1)
    return kept, const, np.tile(np.arange(S, dtype=np.float32), (P, 1)), spread.reshape(16, 8 * P).astype(np.float32), hot


def col(v):
    return v.reshape(-1, P).T


def chunks(w, width=256):
    kt = w.shape[0] // P
    return np.ascontiguousarray(w.reshape(kt, P, -1, width).transpose(2, 1, 0, 3).reshape(-1, P, kt * width))


def lay_out(a):
    w = a["w_in"][0]
    cut = np.cumsum([0, 256, 64, 64, 64, 64, 64, 64, 12, 256, 256, 256, 256, 256, 256, 256, 256, 256])
    qa, kca, vca, ksa, vsa, kwa, vwa, gta, cvb, cvc, cvu, qc, kc, vc, qd, kd, vd = (
        w[:, cut[i]:cut[i + 1]] for i in range(17))
    feature = np.concatenate([qa, kca, vca, ksa, kwa, cvb, cvc, cvu, qc, kc, qd, kd], axis=1)
    w2 = a["w_in_2"][0]
    gate, up = a["w_gate"][0].reshape(D, FT, P), a["w_up"][0].reshape(D, FT, P)
    val2, gate2 = (a["w_up_2"][0][:, FF * i:FF * i + FF].reshape(D, FT, P) for i in range(2))

    def halves(v):
        return np.ascontiguousarray(v.reshape(2, HALF, P, KT, P).transpose(3, 0, 2, 1, 4).reshape(16, P, HALF * P))

    def two(v):
        return np.tile(v.reshape(HD, 1), (2, 1))

    def rows(v):
        return np.tile(v.reshape(1, -1), (P, 1))

    def cmp_w1(v):
        return np.ascontiguousarray(v.reshape(16, P, 256).transpose(1, 0, 2).reshape(P, 16 * 256))

    pe = np.concatenate([a["pe_k_cmp"][0].reshape(16, 2, HD).transpose(2, 1, 0).reshape(HD, 32),
                         a["pe_v_cmp"][0].reshape(16, 2, HD).transpose(2, 1, 0).reshape(HD, 32)], axis=0)
    w2k = a["w2_k_cmp"][0].reshape(2, P, HD).transpose(1, 0, 2)
    w2v = a["w2_v_cmp"][0].reshape(2, P, HD).transpose(1, 0, 2)
    gq, gqd, gkd = two(a["g_q_nsa"]), two(a["g_q_dil"]), two(a["g_k_dil"])
    gkk = np.concatenate([a["g_k_slc"].reshape(HD, 1), a["g_k_win"].reshape(HD, 1)], axis=0)
    convw2 = a["conv_w_2"][0].reshape(3, 2, FT, P).transpose(3, 2, 1, 0).reshape(P, 132)
    convb2 = a["conv_b_2"][0].reshape(2, FT, P).transpose(2, 1, 0).reshape(P, 44)
    gq2, gk2 = two(a["q_norm_w_2"]), two(a["k_norm_w_2"])
    parts = {"g_mix": col(a["g_mix"]), "g_ffn": col(a["g_ffn"]),
             "g_heads": np.concatenate([gq, gq, gkk, gqd, gqd, gkd, gkd], axis=1), "g_kcmp": two(a["g_k_cmp"]),
             "g_out": col(a["g_out"]), "conv": a["conv_w"][0].reshape(3, 2, P).transpose(2, 1, 0).reshape(P, 6),
             "pe": pe, "b_gate": np.tile(rows(a["b_gate"]), (1, NT)),
             "w2k": np.concatenate([w2k, w2k], axis=2).reshape(P, 256), "w2v": w2v.reshape(P, 128),
             "c": col(a["c_2"]), "b_mod": col(a["b_mod_2"]),
             "norm1": col(a["norm1_w_2"]), "norm2": col(a["norm2_w_2"]), "lam_re": col(a["lam_re_2"]),
             "lam_im": col(a["lam_im_2"]), "log_dt": col(np.repeat(a["log_dt_2"][0], 64)),
             "d_skip": col(a["ssm_d_2"]), "b_glu": col(a["b_glu_2"]),
             "g_heads2": np.concatenate([gq2, gq2, gq2, gq2, gk2], axis=1), "sinks": rows(a["sinks_2"]),
             "o_ssm": col(a["out_norm_ssm_2"]), "o_attn": col(a["out_norm_attn_2"]),
             "convw2": convw2, "convb2": convb2}
    assert list(parts) == list(PARAM) and all(v.shape == (P, PARAM[n][1] - PARAM[n][0]) for n, v in parts.items())

    def ssm_b(v):
        out = np.zeros((P, 4, P), v.dtype)
        for g in range(32):
            i = g // 2
            r = 32 * (i % 4) + 16 * (g % 2)
            out[r:r + 16, i // 4, 64 * (g % 2):64 * (g % 2) + 64] = v[g].T
        return out.reshape(P, 512)

    def ssm_c(v):
        out = np.zeros((P, 16, 32), v.dtype)
        for g in range(32):
            out[64 * (g % 2):64 * (g % 2) + 64, g // 2, 16 * (g % 2):16 * (g % 2) + 16] = v[g].T
        return out.reshape(P, 512)

    kept, const, time, spread, hot = constants()
    ones_row = np.ones((1, 8), a["rel_bias_2"].dtype)
    return {
        "x": np.ascontiguousarray(a["x"][0].T.reshape(KT, P, S).transpose(1, 0, 2)),
        "kept": kept, "const": const, "time": time, "spread": spread, "hot": hot,
        "rel_bias": np.concatenate([a["rel_bias_2"], ones_row], axis=0),
        "param": np.ascontiguousarray(np.concatenate([parts[n] for n in PARAM], axis=1)),
        "w_in_f": chunks(feature), "w_in_t": chunks(np.concatenate([vc, vd], axis=1)),
        "w_in_g": chunks(np.concatenate([vsa, vwa, gta], axis=1), 140)[0],
        "w1k": cmp_w1(a["w1_k_cmp"][0]), "w1v": cmp_w1(a["w1_v_cmp"][0]),
        "w_out": chunks(a["w_out"][0]),
        "w_gu": chunks(np.stack([gate, up], axis=2).reshape(D, 2 * FF)),
        "w_down": halves(a["w_down"][0]),
        "w_mod": chunks(a["w_mod_2"][0], 384),
        "w_in2": chunks(w2), "w_glu": chunks(a["w_glu_2"][0], 512)[0],
        "ssm_b": np.concatenate([ssm_b(a["ssm_b_re_2"][0]), ssm_b(a["ssm_b_im_2"][0])], axis=1),
        "ssm_c": np.concatenate([ssm_c(a["ssm_c_re_2"][0]), ssm_c(a["ssm_c_im_2"][0])], axis=1),
        "w_out2": chunks(a["w_out_2"][0]),
        "w_up2": chunks(np.stack([val2, gate2], axis=2).reshape(D, 2 * FF)),
        "w_down2": halves(a["w_down_2"][0]),
    }


def kernel(**inputs):
    import concourse.bacc as _bacc
    from concourse.bass_utils import run_bass_kernel_spmd as _run

    nc = _bacc.Bacc("TRN2", target_bir_lowering=False, num_devices=1)
    arrays = lay_out({name: np.asarray(v) for name, v in inputs.items()})
    io = {name: nc.dram_tensor(f"in_{name}", v.shape, F, kind="ExternalInput").ap() for name, v in arrays.items()}
    io["out"] = nc.dram_tensor("out_x", (P, KT, S), F, kind="ExternalOutput").ap()
    io["rel_scratch"] = nc.dram_tensor("rel_scratch", (8, P, 384), F, kind="Internal").ap()
    program(nc, io)
    r = _run(nc, [{f"in_{name}": v for name, v in arrays.items()}], core_ids=[0])
    return r.results[0]["out_x"].transpose(2, 1, 0).reshape(1, S, D)
```
